# Optimizing a Trainium2 kernel written in Bass

```python
import jax, jax.numpy as jnp
from jax import lax
import numpy as np

D_MODEL = 2048
BATCH = 1
SEQ = 256
DEPTH = 2

N_META = 16
FNET_HEADS = 4
FNET_HEAD_DIM = D_MODEL // 8
FNET_WIDTH = FNET_HEADS * FNET_HEAD_DIM
CONV_HEADS = 4
CONV_HEAD_DIM = D_MODEL // 8
CONV_WIDTH = CONV_HEADS * CONV_HEAD_DIM
CONV_KERNEL = 31
SC_WIDTH = D_MODEL
SC_KERNEL = 3
D_FF = 4 * D_MODEL
N_EVEN = (DEPTH + 1) // 2
N_ODD = DEPTH // 2
AB_IN = FNET_WIDTH + 2 * CONV_WIDTH
AB_OUT = FNET_WIDTH + CONV_WIDTH
EPS = 1e-6

kernel_name = "hybrid_fnet_conformer_shortconv_encoder"

def rms_norm(x, g):
    xf = x.astype(jnp.float32)
    y = xf * lax.rsqrt(jnp.mean(xf * xf, axis=-1, keepdims=True) + EPS)
    return (y * g.astype(jnp.float32)).astype(x.dtype)

def depthwise_conv_centred(h, w):
    k = w.shape[0]
    pad = (k - 1) // 2
    return lax.conv_general_dilated(
        h, w[:, None, :].astype(h.dtype), window_strides=(1,),
        padding=[(pad, pad)], dimension_numbers=("NWC", "WIO", "NWC"),
        feature_group_count=h.shape[-1])

def fourier_mix(u):
    f = jnp.fft.fft2(u.astype(jnp.float32), axes=(1, 3), norm="ortho")
    return jnp.real(f).astype(u.dtype)

def conformer_conv(v, conv_w, conv_b, ln_g, ln_b):
    a, gate = jnp.split(v, 2, axis=-1)
    h = a * jax.nn.sigmoid(gate)
    h = depthwise_conv_centred(h, conv_w) + conv_b.astype(h.dtype)
    b_, l_, _ = h.shape
    hg = h.reshape(b_, l_, CONV_HEADS, CONV_HEAD_DIM).astype(jnp.float32)
    mu = jnp.mean(hg, axis=-1, keepdims=True)
    var = jnp.mean(jnp.square(hg - mu), axis=-1, keepdims=True)
    hg = ((hg - mu) * lax.rsqrt(var + EPS)).reshape(b_, l_, CONV_WIDTH)
    hg = hg * ln_g.astype(jnp.float32) + ln_b.astype(jnp.float32)
    return jax.nn.silu(hg).astype(v.dtype)

def even_mixer(xn, w_in, w_out, conv_w, conv_b, ln_g, ln_b):
    b_, l_, _ = xn.shape
    proj = xn @ w_in
    u = proj[..., :FNET_WIDTH]
    v = proj[..., FNET_WIDTH:]
    ya = fourier_mix(u.reshape(b_, l_, FNET_HEADS, FNET_HEAD_DIM)).reshape(b_, l_, FNET_WIDTH)
    yb = conformer_conv(v, conv_w, conv_b, ln_g, ln_b)
    return jnp.concatenate([ya, yb], axis=-1) @ w_out

def odd_mixer(xn, w_in, conv_w, w_out):
    gb, gc, hin = jnp.split(xn @ w_in, 3, axis=-1)
    y = gb * depthwise_conv_centred(gc * hin, conv_w)
    return y @ w_out

def sq_relu_mlp(xn, w1, w2):
    return jnp.square(jax.nn.relu(xn @ w1)) @ w2

def setup_inputs(seed: int = 0) -> dict:
    key = jax.random.key(seed)
    ks = jax.random.split(key, 20)
    nrm = jax.random.normal
    f32 = jnp.float32
    d = D_MODEL
    return {
        "x": nrm(ks[0], (BATCH, SEQ, d), f32),
        "meta_tokens": nrm(ks[1], (N_META, d), f32),
        "norm_mix_g": 1.0 + 0.02 * nrm(ks[2], (DEPTH, d), f32),
        "norm_mlp_g": 1.0 + 0.02 * nrm(ks[3], (DEPTH, d), f32),
        "norm_final_g": 1.0 + 0.02 * nrm(ks[4], (d,), f32),
        "ab_w_in": nrm(ks[5], (N_EVEN, d, AB_IN), f32) * d ** -0.5,
        "ab_w_out": nrm(ks[6], (N_EVEN, AB_OUT, d), f32) * AB_OUT ** -0.5,
        "ab_conv_w": nrm(ks[7], (N_EVEN, CONV_KERNEL, CONV_WIDTH), f32) * CONV_KERNEL ** -0.5,
        "ab_conv_b": 0.01 * nrm(ks[8], (N_EVEN, CONV_WIDTH), f32),
        "ab_ln_g": 1.0 + 0.02 * nrm(ks[9], (N_EVEN, CONV_WIDTH), f32),
        "ab_ln_b": 0.01 * nrm(ks[10], (N_EVEN, CONV_WIDTH), f32),
        "c_w_in": nrm(ks[11], (N_ODD, d, 3 * SC_WIDTH), f32) * d ** -0.5,
        "c_conv_w": nrm(ks[12], (N_ODD, SC_KERNEL, SC_WIDTH), f32) * SC_KERNEL ** -0.5,
        "c_w_out": nrm(ks[13], (N_ODD, SC_WIDTH, d), f32) * SC_WIDTH ** -0.5,
        "mlp_w1": nrm(ks[14], (DEPTH, d, D_FF), f32) * d ** -0.5,
        "mlp_w2": nrm(ks[15], (DEPTH, D_FF, d), f32) * D_FF ** -0.5,
    }

def reference(x, meta_tokens, norm_mix_g, norm_mlp_g, norm_final_g,
              ab_w_in, ab_w_out, ab_conv_w, ab_conv_b, ab_ln_g, ab_ln_b,
              c_w_in, c_conv_w, c_w_out, mlp_w1, mlp_w2):
    b_ = x.shape[0]
    meta = jnp.broadcast_to(meta_tokens[None].astype(x.dtype), (b_, N_META, D_MODEL))
    h = jnp.concatenate([meta, x], axis=1)
    for layer in range(DEPTH):
        hn = rms_norm(h, norm_mix_g[layer])
        i = layer // 2
        if layer % 2 == 0:
            h = h + even_mixer(hn, ab_w_in[i], ab_w_out[i], ab_conv_w[i],
                               ab_conv_b[i], ab_ln_g[i], ab_ln_b[i])
        else:
            h = h + odd_mixer(hn, c_w_in[i], c_conv_w[i], c_w_out[i])
        h = h + sq_relu_mlp(rms_norm(h, norm_mlp_g[layer]), mlp_w1[layer], mlp_w2[layer])
    h = rms_norm(h, norm_final_g)
    return h[:, N_META:, :]


_drawn_inputs = setup_inputs


def setup_inputs(seed=0):
    import zlib

    import numpy as np

    out = dict(_drawn_inputs(seed))
    spreads = {}
    factors = {'norm_final_g': 8.161,
     'ab_conv_b': 6.285,
     'ab_ln_g': 4.769,
     'ab_ln_b': 26.333,
     'norm_mlp_g': 4.056}
    for name, (base, spread) in spreads.items():
        noise = np.random.default_rng([zlib.crc32(name.encode()), seed]).standard_normal(out[name].shape)
        drawn = base * np.exp(spread * noise) if base else spread * noise
        out[name] = __import__('jax').numpy.asarray(drawn.astype(out[name].dtype))
    for name, factor in factors.items():
        out[name] = (out[name] * factor).astype(out[name].dtype)
    return out
```

```python
from contextlib import ExitStack

import numpy as np
import concourse.bass as bass
from concourse import mybir

F32 = mybir.dt.float32
F32R = mybir.dt.float32r
ALU = mybir.AluOpType
ACT = mybir.ActivationFunctionType

P = 128
D = 2048
META, SEQ = 16, 256
L = META + SEQ
DFF = 4 * D
KT = D // P
HEADS, HEAD_DIM = 4, D // 8
TAPS, PAD = 31, 15
CONV_TILES = HEADS * HEAD_DIM // P
EPS = 1e-6

COLS = 512
M = COLS // P
CHUNK_K = 4
SLAB_K = 2
SLABS = KT // SLAB_K
RAW = 4
RING = 4

FROM1 = META - 2
FROM2 = META
N0, N1, N2 = L, L - FROM1, L - FROM2

G_IN, G_OUT_A, G_OUT_B, G_MLP0 = 0, 6, 10, 14
G_C_IN, G_C_OUT, G_MLP1, G_END = 46, 58, 62, 94
S_IN, S_OUT_A, S_OUT_B, S_MLP0 = 0, 48, 64, 80
S_C_IN, S_C_OUT, S_MLP1, S_END = 336, 432, 464, 720
CHUNKS = S_END // 2
QUARTERS = 4
GQ, SQ = 8, 64

C_GAIN = 0
C_CONV = C_GAIN + 5 * KT
C_BIAS = C_CONV + CONV_TILES * TAPS
C_LNG = C_BIAS + CONV_TILES
C_LNB = C_LNG + CONV_TILES
C_SHORT = C_LNB + CONV_TILES
C_END = C_SHORT + KT * 3

TOK = 96
TOK_AT = (0, TOK, L - TOK)


def trunk(nc, weights, x, params, dft_ch, dft_seq, out):
    with ExitStack() as ctx:
        def sb(name, shape, dt=F32):
            return ctx.enter_context(nc.sbuf_tensor(name, shape, dt))

        def sem(name):
            return ctx.enter_context(nc.semaphore(name))

        h = sb("h", [P, KT, L])
        xs = sb("xs", [P, 2 * KT * L], F32R)
        hid = sb("hid", [P, 2, KT, L], F32R)
        raw = sb("raw", [P, RAW, CHUNK_K * COLS])
        wh = sb("wh", [P, RING, SLAB_K, COLS], F32R)
        wl = sb("wl", [P, RING, SLAB_K, COLS], F32R)
        rstd = sb("rstd", [P, L])
        act4 = sb("act4", [P, M, L])
        sq4 = sb("sq4", [P, M, L])
        ssum = sb("ssum", [P, M, L])
        par = sb("par", [P, C_END])
        ones = sb("ones", [P, P])
        eps = sb("eps", [P, 1])
        conv_in = sb("conv_in", [P, CONV_TILES, L + 2 * PAD])
        conv = sb("conv", [P, CONV_TILES, L])
        tch = sb("tch", [P, 2, SLAB_K * COLS], F32R)
        tseq = sb("tseq", [TOK, 2, 3 * 2 * L], F32R)

        xs4 = xs[:, :].rearrange("p (s k l) -> p s k l", s=2, k=KT)
        vs = xs[:, 0:2 * 2 * 3 * COLS].rearrange("p (b s t c) -> p b s t c", b=2, s=2, t=3)
        tch4 = tch[:, :, :].rearrange("p s (k c) -> p s k c", k=SLAB_K)
        tseq4 = tseq[:, :, :].rearrange("p s (t f l) -> p s t f l", t=3, f=2)
        raw_ch = act4[:, :, :].rearrange("p m l -> p (m l)")[:, 0:SLAB_K * COLS]
        raw_seq = conv[:, :, :].rearrange("p m l -> p (m l)")[0:TOK, 0:3 * 2 * L]
        flat_conv = conv[:, :, :].rearrange("p m l -> p (m l)")
        gate_c = flat_conv[:, 0:M * N1].rearrange("p (m l) -> p m l", m=M)
        short_out = flat_conv[:, M * N1:M * (N1 + N2)].rearrange("p (m l) -> p m l", m=M)
        short_in = conv_in[:, 0:M, 0:N1 + 1]

        banks = ctx.enter_context(nc.psum_tensor("banks", [P, 2 * M, COLS], F32))

        raw_landed = [sem(f"raw_landed{i}") for i in range(RAW)]
        x_landed = [sem(f"x_landed{i}") for i in range(KT // M)]
        par_landed = sem("par_landed")
        ch_landed = sem("ch_landed")
        seq_landed = sem("seq_landed")
        stored = sem("stored")
        consts_set = sem("consts_set")
        high_ready = sem("high_ready")
        low_ready = sem("low_ready")
        slab_used = sem("slab_used")
        banks_free = sem("banks_free")
        x_high = sem("x_high")
        x_ready = sem("x_ready")
        squared = sem("squared")
        summed = sem("summed")
        ssum_ready = sem("ssum_ready")
        total_ready = sem("total_ready")
        root_ready = sem("root_ready")
        rstd_ready = sem("rstd_ready")
        glu_sig = sem("glu_sig")
        glu_ready = sem("glu_ready")
        u_high = sem("u_high")
        u_ready = sem("u_ready")
        table_high = sem("table_high")
        table_ready = sem("table_ready")
        ch_done = sem("ch_done")
        v_high = sem("v_high")
        v_ready = sem("v_ready")
        seq_done = sem("seq_done")
        ya_high = sem("ya_high")
        ya_ready = sem("ya_ready")
        tap_done = sem("tap_done")
        ln_sum = sem("ln_sum")
        ln_mean = sem("ln_mean")
        ln_centred = sem("ln_centred")
        ln_sq = sem("ln_sq")
        ln_sqsum = sem("ln_sqsum")
        ln_var = sem("ln_var")
        ln_root = sem("ln_root")
        ln_rstd = sem("ln_rstd")
        ln_normed = sem("ln_normed")
        ln_sig = sem("ln_sig")
        ln_affine = sem("ln_affine")
        ln_out = sem("ln_out")
        yb_high = sem("yb_high")
        yb_ready = sem("yb_ready")
        relu_sq = sem("relu_sq")
        relu_high = sem("relu_high")
        hid_ready = sem("hid_ready")
        short_ready = sem("short_ready")
        short_tap = sem("short_tap")
        y_ready = sem("y_ready")
        y_high = sem("y_high")
        gated_ready = sem("gated_ready")
        scaled = sem("scaled")
        normed = sem("normed")

        block = ctx.enter_context(nc.Block())

        def psum(parity, n):
            return banks[:, M * parity:M * parity + M, 0:n]

        def tiles(t, g, lo):
            return t[:, M * g:M * g + M, lo:L]

        def over(tok, n_tiles, lo=0):
            return tok[:, lo:L].unsqueeze(1).broadcast_to([P, n_tiles, L - lo])

        def ch_bank(hd):
            return 5 * (hd % 2)

        def seq_bank(hd):
            return 3 if hd < 3 else 5

        def seq_psum(hd):
            return banks[:, seq_bank(hd):seq_bank(hd) + 2, 0:N1]

        def gain(norm, tile):
            return par[:, C_GAIN + norm * KT + tile:C_GAIN + norm * KT + tile + 1]

        @block.sync
        def _(sp):
            def load_chunk(n, slot, refill):
                if refill:
                    sp.wait_ge(low_ready, (n - RAW + 1) * 2)
                src = weights[n, :, :] if isinstance(n, int) else weights[bass.ds(n, 1), :, :]
                if not isinstance(n, int):
                    src = src.rearrange("a p c -> p (a c)")
                sp.dma_start(raw[:, slot, :], src).then_inc(raw_landed[slot], 16)

            for q in range(KT // M):
                sp.dma_start(h[:, M * q:M * q + M, :], x[:, M * q:M * q + M, :]).then_inc(x_landed[q], 16)
                load_chunk(q, q, False)
            with sp.Fori(1, CHUNKS // RAW) as r:
                for slot in range(RAW):
                    load_chunk(r * RAW + slot, slot, True)
            for g in range(KT // M):
                sp.wait_ge(normed, g + 1)
                sp.dma_start(out[:, M * g:M * g + M, :], tiles(h, g, FROM2)).then_inc(stored, 16)
            sp.wait_ge(stored, 16 * (KT // M))

        @block.gpsimd
        def _(pool):
            pool.dma_start(par[:, :], params).then_inc(par_landed, 16)
            pool.dma_start(raw_ch, dft_ch).then_inc(ch_landed, 16)
            pool.dma_start(raw_seq, dft_seq).then_inc(seq_landed, 16)
            pool.memset(ones[:, :], 1.0).then_inc(consts_set, 1)
            pool.memset(eps[:, :], EPS).then_inc(consts_set, 1)
            pool.memset(conv_in[:, :, 0:PAD], 0.0).then_inc(consts_set, 1)
            pool.memset(conv_in[:, :, PAD + L:], 0.0).then_inc(consts_set, 1)

            def sum_squares(norm, lo):
                for q in range(KT // M):
                    done = norm * (KT // M) + q
                    pool.wait_ge(squared, done + 1)
                    if q == 0:
                        if norm:
                            pool.wait_ge(total_ready, norm)
                        pool.tensor_copy(ssum[:, :, lo:], sq4[:, :, lo:]).then_inc(summed, 1)
                    else:
                        pool.wait_ge(summed, done)
                        pool.tensor_tensor(ssum[:, :, lo:], ssum[:, :, lo:], sq4[:, :, lo:],
                                           ALU.add).then_inc(summed, 1)
                pool.wait_ge(summed, (norm + 1) * (KT // M))
                pool.tensor_tensor(ssum[:, 0:2, lo:], ssum[:, 0:2, lo:], ssum[:, 2:4, lo:],
                                   ALU.add).then_inc(ssum_ready, 1)
                pool.wait_ge(ssum_ready, 2 * norm + 1)
                pool.tensor_tensor(ssum[:, 0, lo:], ssum[:, 0, lo:], ssum[:, 1, lo:],
                                   ALU.add).then_inc(ssum_ready, 1)

            def fold(dst, src, wait, count, done):
                pool.wait_ge(wait, count)
                pool.tensor_tensor(dst, src[0], src[1], ALU.add).then_inc(done, 1)

            sum_squares(0, 0)
            pool.wait_ge(total_ready, 1)
            def head_sum(hd):
                fold(ssum[:, hd, FROM1:], [conv[:, 2 * hd + i, FROM1:] for i in range(2)],
                     tap_done, (hd + 1) * 2 * TAPS, ln_sum)

            def head_sqsum(hd):
                pool.wait_ge(ln_mean, hd + 1)
                fold(ssum[:, hd, FROM1:], [sq4[:, 2 * (hd % 2) + i, FROM1:] for i in range(2)],
                     ln_sq, hd + 1, ln_sqsum)

            for hd in range(3):
                head_sum(hd)
            for hd in range(3):
                head_sqsum(hd)
            head_sum(3)
            head_sqsum(3)
            pool.wait_ge(ln_var, HEADS)
            sum_squares(1, FROM1)
            sum_squares(2, FROM1)
            sum_squares(3, FROM2)
            sum_squares(4, FROM2)

        @block.tensor
        def _(pe):
            def product(dst, w, v, start, stop):
                pe.matmul(dst, w[0], v[0], start=start, stop=False)
                pe.matmul(dst, w[0], v[1], start=False, stop=False)
                return pe.matmul(dst, w[1], v[0], start=False, stop=stop)

            def group(slab0, index, parity, moving, lo, n_slabs=SLABS, tile0=0, ready=None, side=None):
                if not isinstance(index, int) or index >= 2:
                    pe.wait_ge(banks_free, index - 1)
                for s in range(n_slabs):
                    pe.wait_ge(low_ready, slab0 + (s + 1))
                    if ready:
                        ready(s)
                    for m in range(M):
                        for t in range(SLAB_K):
                            k = tile0 + SLAB_K * s + t
                            slot = s % RING
                            cols = slice(P * m, P * m + P)
                            last = product(banks[:, M * parity + m, 0:L - lo],
                                           (wh[:, slot, t, cols], wl[:, slot, t, cols]),
                                           (moving[:, 0, k, lo:L], moving[:, 1, k, lo:L]),
                                           s + t == 0, s == n_slabs - 1 and t == SLAB_K - 1)
                    last.then_inc(slab_used, 1)
                    if side and s in side:
                        side[s]()

            def x_tiles(norm):
                return lambda s: s % 2 == 0 and pe.wait_ge(x_ready, norm * (KT // M) + s // 2 + 1)

            def norm_total(norm, lo):
                def run():
                    pe.wait_ge(ssum_ready, 2 * norm + 2)
                    if norm:
                        pe.wait_ge(banks_free, (G_IN, G_MLP0, G_C_IN, G_MLP1, G_END)[norm])
                    bank = M if norm < 4 else 0
                    pe.matmul(banks[:, bank, 0:L - lo], ones[:, :], ssum[:, 0, lo:],
                              start=True, stop=True).then_inc(total_ready, 1)
                return run

            def x_phase(slab0, index0, pairs, norm, lo):
                group(slab0, index0, 0, xs4, lo, ready=x_tiles(norm), side={5: norm_total(norm, lo)})
                pe.wait_ge(root_ready, norm + 1)
                group(slab0 + SLABS, index0 + 1, 1, xs4, lo)
                if pairs > 1:
                    with pe.Fori(1, pairs) as i:
                        for par_ in range(2):
                            group(i * (2 * SLABS) + (slab0 + SLABS * par_), i * 2 + (index0 + par_),
                                  par_, xs4, lo)

            def hid_phase(slab0, index0, pairs, lo, ready):
                with pe.Fori(0, pairs) as i:
                    for par_ in range(2):
                        group(i * (2 * SLABS) + (slab0 + SLABS * par_), i * 2 + (index0 + par_),
                              par_, hid, lo, ready=ready)

            def mlp(slab0, index0, norm, lo, hid0):
                x_phase(slab0, index0, 2, norm, lo)
                hid_phase(slab0 + SQ // 2, index0 + GQ // 2, 2, lo,
                          lambda s: s % 2 == 0 and pe.wait_ge(hid_ready, hid0 + s // 2 + 1))
                with pe.Fori(1, QUARTERS) as q:
                    with pe.Fori(0, 2) as i:
                        for par_ in range(2):
                            group(q * SQ + i * (2 * SLABS) + (slab0 + SLABS * par_),
                                  q * GQ + i * 2 + (index0 + par_), par_, xs4, lo)
                    with pe.Fori(0, 2) as i:
                        for par_ in range(2):
                            group(q * SQ + i * (2 * SLABS) + (slab0 + SQ // 2 + SLABS * par_),
                                  q * GQ + i * 2 + (index0 + GQ // 2 + par_), par_, hid, lo,
                                  ready=lambda s: s % 2 == 0 and pe.wait_ge(
                                      hid_ready, q * 4 + (hid0 + s // 2 + 1)))

            def channel_dft(hd):
                pe.wait_ge(u_ready, hd // 2 + 1)
                if hd < 2:
                    pe.wait_ge(banks_free, G_OUT_A - 1 + hd)
                for t, at in enumerate(TOK_AT):
                    for k in range(2):
                        u = hid[:, :, KT // 2 + 2 * hd + k, at:at + TOK]
                        last = product(banks[0:TOK, ch_bank(hd) + t, :], (u[:, 0], u[:, 1]),
                                       (tch4[:, 0, k], tch4[:, 1, k]), k == 0, k == 1)
                last.then_inc(ch_done, 1)

            def sequence_dft(hd):
                pe.wait_ge(v_ready, hd + 1)
                if hd:
                    pe.wait_ge(ya_ready, hd)
                for j in range(2):
                    for f in range(2):
                        for t in range(3):
                            cols = slice(HEAD_DIM * f + P * j, HEAD_DIM * f + P * j + P)
                            v = vs[0:TOK, hd % 2, :, t, cols]
                            last = product(banks[:, seq_bank(hd) + j, 0:N1], (v[:, 0], v[:, 1]),
                                           (tseq4[:, 0, t, f, FROM1:], tseq4[:, 1, t, f, FROM1:]),
                                           f + t == 0, f == 1 and t == 2)
                last.then_inc(seq_done, 1)

            def ln_total(hd, bank, ready, done):
                pe.wait_ge(ready, hd + 1)
                pe.matmul(banks[:, bank, 0:N1], ones[:, :], ssum[:, hd, FROM1:],
                          start=True, stop=True).then_inc(done, 1)

            pe.wait_ge(consts_set, 4)
            x_phase(S_IN, G_IN, 3, 0, 0)

            pe.wait_ge(table_ready, 2)
            channel_dft(0)
            channel_dft(1)
            sequence_dft(0)
            channel_dft(2)
            sequence_dft(1)
            channel_dft(3)
            sequence_dft(2)
            sequence_dft(3)

            def means_first():
                pe.wait_ge(ya_ready, HEADS)
                for hd in range(3):
                    ln_total(hd, M + hd, ln_sum, ln_mean)

            def variances_first():
                pe.wait_ge(banks_free, G_OUT_A + 1)
                for hd in range(3):
                    ln_total(hd, hd, ln_sqsum, ln_var)
                ln_total(3, 3, ln_sum, ln_mean)

            def variance_last():
                pe.wait_ge(banks_free, G_OUT_A + 2)
                ln_total(3, M, ln_sqsum, ln_var)

            HALF = SLABS // 2
            sides = [{1: means_first}, {2: variances_first}, {2: variance_last}, None]
            for g in range(4):
                if g == 1:
                    pe.wait_ge(ln_centred, 3)
                if g == 2:
                    pe.wait_ge(ln_root, 3)
                    pe.wait_ge(ln_centred, 4)
                if g == 3:
                    pe.wait_ge(ln_root, 4)
                ready = (lambda s: pe.wait_ge(ya_ready, s + 1)) if g == 0 else None
                group(S_OUT_A + HALF * g, G_OUT_A + g, g % 2, hid, FROM1, n_slabs=HALF, ready=ready,
                      side=sides[g])
            for g in range(4):
                ready = (lambda s: pe.wait_ge(yb_ready, s + 1)) if g == 0 else None
                group(S_OUT_B + HALF * g, G_OUT_B + g, g % 2, hid, FROM1, n_slabs=HALF,
                      tile0=KT // 2, ready=ready)

            mlp(S_MLP0, G_MLP0, 1, FROM1, 0)

            x_phase(S_C_IN, G_C_IN, 6, 2, FROM1)
            hid_phase(S_C_OUT, G_C_OUT, 2, FROM2,
                      lambda s: s % 2 == 0 and pe.wait_ge(gated_ready, s // 2 + 1))
            mlp(S_MLP1, G_MLP1, 3, FROM2, QUARTERS * 4)
            norm_total(4, FROM2)()

        @block.scalar
        def _(act):
            def high(slab0, j):
                slab, chunk_slot = slab0 + j, (j // 2) % RAW
                if j % 2 == 0:
                    loads = j // (2 * RAW) + 1
                    act.wait_ge(raw_landed[chunk_slot], slab0 * (16 // (2 * RAW)) + 16 * loads)
                if not isinstance(slab, int) or slab >= RING:
                    act.wait_ge(slab_used, slab - (RING - 1))
                src = raw[:, chunk_slot, SLAB_K * COLS * (j % 2):SLAB_K * COLS * (j % 2 + 1)]
                act.activation(wh[:, j % RING, :, :], src.rearrange("p (t c) -> p t c", t=SLAB_K),
                               ACT.Copy).then_inc(high_ready, 1)

            def slabs(slab0, lo, hi):
                for j in range(lo, hi):
                    high(slab0, j)

            def split_x(norm, g, lo, residual=None):
                if residual is not None:
                    act.wait_ge(banks_free, residual)
                for t in range(M * g, M * g + M):
                    act.activation(xs4[:, 0, t, lo:], h[:, t, lo:], ACT.Copy,
                                   scale=gain(norm, t)).then_inc(x_high, 1)
                square(norm, g, lo)

            def square(norm, g, lo):
                n = norm * (KT // M) + g
                if n:
                    act.wait_ge(summed, n)
                act.activation(sq4[:, :, lo:], tiles(h, g, lo), ACT.Square).then_inc(squared, 1)

            def norm_root(norm, lo):
                act.wait_ge(total_ready, norm + 1)
                bank = M if norm < 4 else 0
                act.activation(rstd[:, lo:], banks[:, bank, 0:L - lo], ACT.Sqrt,
                               bias=eps[:, :], scale=1.0 / D).then_inc(root_ready, 1)

            def relu_split(r, index, g, lo):
                act.wait_ge(banks_free, index + 1)
                act.activation(sq4[:, :, lo:], act4[:, :, lo:], ACT.Square).then_inc(relu_sq, 1)
                act.wait_ge(relu_sq, r + 1)
                act.activation(tiles(hid[:, 0], g, lo), sq4[:, :, lo:], ACT.Copy).then_inc(relu_high, 1)

            def glu(g):
                act.wait_ge(banks_free, g + 1)
                act.activation(sq4[:, 0:2, :], act4[:, 2:4, :], ACT.Sigmoid).then_inc(glu_sig, 1)

            def split_u(g):
                act.wait_ge(banks_free, 5 + g)
                act.activation(tiles(hid[:, 0], 2 + g, 0), act4[:, :, :], ACT.Copy).then_inc(u_high, 1)

            def split_v(hd):
                act.wait_ge(ch_done, hd + 1)
                act.activation(vs[0:TOK, hd % 2, 0, :, :], banks[0:TOK, ch_bank(hd):ch_bank(hd) + 3, :],
                               ACT.Copy).then_inc(v_high, 1)

            def split_ya(hd):
                act.wait_ge(seq_done, hd + 1)
                act.activation(hid[:, 0, 2 * hd:2 * hd + 2, FROM1:], seq_psum(hd), ACT.Copy).then_inc(ya_high, 1)

            def head_tiles(hd):
                return conv[:, 2 * hd:2 * hd + 2, FROM1:]

            def ln_square(hd):
                act.wait_ge(ln_centred, hd + 1)
                if hd >= 2:
                    act.wait_ge(ln_sqsum, hd - 1)
                act.activation(sq4[:, 2 * (hd % 2):2 * (hd % 2) + 2, FROM1:], head_tiles(hd),
                               ACT.Square).then_inc(ln_sq, 1)

            def ln_roots(hd, bank):
                act.wait_ge(ln_var, hd + 1)
                act.activation(act4[:, hd, FROM1:], banks[:, bank, 0:N1], ACT.Sqrt,
                               bias=eps[:, :], scale=1.0 / HEAD_DIM).then_inc(ln_root, 1)

            def ln_silu(hd):
                act.wait_ge(ln_normed, hd + 1)
                if hd == 0:
                    act.wait_ge(ln_sqsum, HEADS)
                if hd >= 2:
                    act.wait_ge(ln_out, hd - 1)
                for i in range(2):
                    t = 2 * hd + i
                    act.activation(sq4[:, 2 * (hd % 2) + i, FROM1:], conv[:, t, FROM1:], ACT.Sigmoid,
                                   bias=par[:, C_LNB + t:C_LNB + t + 1],
                                   scale=par[:, C_LNG + t:C_LNG + t + 1]).then_inc(ln_sig, 1)
                act.wait_ge(ln_sig, 2 * hd + 2)
                for i in range(2):
                    t = 2 * hd + i
                    act.activation(conv[:, t, FROM1:], conv[:, t, FROM1:], ACT.Identity,
                                   bias=par[:, C_LNB + t:C_LNB + t + 1],
                                   scale=par[:, C_LNG + t:C_LNG + t + 1]).then_inc(ln_affine, 1)

            def split_yb(hd):
                act.wait_ge(ln_out, hd + 1)
                act.activation(hid[:, 0, KT // 2 + 2 * hd:KT // 2 + 2 * hd + 2, FROM1:], head_tiles(hd),
                               ACT.Copy).then_inc(yb_high, 1)

            def split_gated(j):
                act.wait_ge(y_ready, j + 1)
                act.activation(tiles(hid[:, 0], j, FROM2), short_out, ACT.Copy).then_inc(y_high, 1)

            E = RING

            act.wait_ge(par_landed, 16)
            for q in range(KT // M):
                act.wait_ge(x_landed[q], 16)
                split_x(0, q, 0)
                slabs(0, q, q + 1)
            act.wait_ge(ch_landed, 16)
            act.activation(tch[:, 0, :], raw_ch, ACT.Copy).then_inc(table_high, 1)
            act.wait_ge(seq_landed, 16)
            act.activation(tseq[:, 0, :], raw_seq, ACT.Copy).then_inc(table_high, 1)
            slabs(0, E, SLABS)
            norm_root(0, 0)
            for g in range(1, 6):
                slabs(SLABS * g, 0, E)
                glu(g - 1) if g < 5 else split_u(0)
                slabs(SLABS * g, E, SLABS)
            split_u(1)
            slabs(S_OUT_A, 0, RING)
            split_v(0)
            split_v(1)
            split_ya(0)
            split_v(2)
            split_ya(1)
            split_v(3)
            split_ya(2)
            split_ya(3)
            slabs(S_OUT_A, 4, 6)
            for hd in range(3):
                ln_square(hd)
            slabs(S_OUT_A, 6, 10)
            for hd in range(3):
                ln_roots(hd, hd)
            slabs(S_OUT_A, 10, 11)
            ln_square(3)
            slabs(S_OUT_A, 11, 14)
            ln_roots(3, M)
            slabs(S_OUT_A, 14, 16)
            for hd in range(HEADS):
                ln_silu(hd)
                split_yb(hd)
                if hd:
                    slabs(S_OUT_B, hd - 1, hd)
            slabs(S_OUT_B, 3, 8)
            split_x(1, 0, FROM1, G_OUT_B + 1)
            slabs(S_OUT_B, 8, 12)
            split_x(1, 1, FROM1, G_OUT_B + 2)
            slabs(S_OUT_B, 12, 16)
            split_x(1, 2, FROM1, G_OUT_B + 3)

            def mlp(slab0, norm, lo, index0, r0, next_norm, next_lo):
                def quarter(q, first=False, last=False):
                    s0, r = q * SQ + slab0, q * 4 + r0
                    for g in range(GQ):
                        slabs(s0, SLABS * g, SLABS * g + E)
                        if g == 0 and first:
                            split_x(norm, 3, lo, index0)
                        if 1 <= g <= 4:
                            relu_split(r + (g - 1), q * GQ + (index0 + g - 1), g - 1, lo)
                        if g > 4 and last:
                            if next_norm < 4:
                                split_x(next_norm, g - 5, next_lo, index0 + 3 * GQ + g)
                            else:
                                act.wait_ge(banks_free, index0 + 3 * GQ + g)
                                square(4, g - 5, next_lo)
                        slabs(s0, SLABS * g + E, SLABS * g + SLABS)
                        if g == 0 and first:
                            norm_root(norm, lo)
                quarter(0, first=True)
                with act.Fori(1, QUARTERS - 1) as q:
                    quarter(q)
                quarter(QUARTERS - 1, last=True)

            mlp(S_MLP0, 1, FROM1, G_MLP0, 0, 2, FROM1)

            def gated_three(i, first=False):
                for k in range(3):
                    s0 = i * (3 * SLABS) + (S_C_IN + SLABS * k)
                    slabs(s0, 0, E)
                    if k == 0:
                        if first:
                            split_x(2, 3, FROM1, G_C_IN)
                        else:
                            split_gated_at(i - 1)
                    slabs(s0, E, SLABS)
                    if k == 0 and first:
                        norm_root(2, FROM1)

            def split_gated_at(j):
                split_gated(j)

            for i in range(4):
                gated_three(i, first=(i == 0))
            for g in range(4):
                slabs(S_C_OUT + SLABS * g, 0, E)
                if g == 0:
                    split_gated(3)
                else:
                    split_x(3, g - 1, FROM2, G_C_OUT + g)
                slabs(S_C_OUT + SLABS * g, E, SLABS)

            mlp(S_MLP1, 3, FROM2, G_MLP1, 4 * QUARTERS, 4, FROM2)
            act.wait_ge(banks_free, G_END)
            square(4, 3, FROM2)
            act.wait_ge(squared, 20)
            for t in range(KT):
                act.activation(h[:, t, FROM2:], h[:, t, FROM2:], ACT.Copy,
                               scale=gain(4, t)).then_inc(scaled, 1)
            norm_root(4, FROM2)

        @block.vector
        def _(dve):
            def low(slab, j):
                dve.wait_ge(high_ready, slab + 1)
                src = raw[:, (j // 2) % RAW, SLAB_K * COLS * (j % 2):SLAB_K * COLS * (j % 2 + 1)]
                dve.tensor_tensor(wl[:, j % RING, :, :], src.rearrange("p (t c) -> p t c", t=SLAB_K),
                                  wh[:, j % RING, :, :].bitcast(F32), ALU.subtract).then_inc(low_ready, 1)

            def slabs(slab0, lo, hi):
                for j in range(lo, hi):
                    low(slab0 + j, j)

            def split_x(norm, g, lo):
                for t in range(M * g, M * g + M):
                    dve.wait_ge(x_high, norm * KT + t + 1)
                    last = dve.scalar_tensor_tensor(xs4[:, 1, t, lo:], h[:, t, lo:], gain(norm, t),
                                                    xs4[:, 0, t, lo:].bitcast(F32), ALU.mult, ALU.subtract)
                last.then_inc(x_ready, 1)

            def group_done(slab_end, index):
                dve.wait_ge(slab_used, slab_end)
                if not isinstance(index, int) or index > 0:
                    dve.wait_ge(banks_free, index)

            def residual(g, slab_end, index, parity, lo):
                group_done(slab_end, index)
                dve.tensor_tensor(tiles(h, g, lo), tiles(h, g, lo), psum(parity, L - lo),
                                  ALU.add).then_inc(banks_free, 1)

            def scale(dst, slab_end, index, lo):
                group_done(slab_end, index)
                dve.tensor_tensor(dst, psum(index % 2, L - lo), over(rstd, M, lo),
                                  ALU.mult).then_inc(banks_free, 1)

            def reciprocal(norm, lo):
                dve.wait_ge(root_ready, norm + 1)
                dve.reciprocal(rstd[:, lo:], rstd[:, lo:]).then_inc(rstd_ready, 1)
                dve.wait_ge(rstd_ready, norm + 1)

            def low_of(dst, src, high_t, wait, count, done):
                dve.wait_ge(wait, count)
                dve.tensor_tensor(dst, src, high_t.bitcast(F32), ALU.subtract).then_inc(done, 1)

            def relu_split(r, g, slab_end, index, parity, lo):
                group_done(slab_end, index)
                dve.scalar_tensor_tensor(act4[:, :, lo:], psum(parity, L - lo), 0.0, over(rstd, M, lo),
                                         ALU.max, ALU.mult).then_inc(banks_free, 1)
                low_of(tiles(hid[:, 1], g, lo), sq4[:, :, lo:], tiles(hid[:, 0], g, lo),
                       relu_high, r + 1, hid_ready)

            def glu(g, slab_end):
                scale(act4[:, :, :], slab_end, g, 0)
                dve.wait_ge(glu_sig, g + 1)
                dve.tensor_tensor(conv_in[:, 2 * g:2 * g + 2, PAD:PAD + L], act4[:, 0:2, :], sq4[:, 0:2, :],
                                  ALU.mult).then_inc(glu_ready, 1)

            def split_u(g, slab_end):
                scale(act4[:, :, :], slab_end, 4 + g, 0)
                low_of(tiles(hid[:, 1], 2 + g, 0), act4[:, :, :], tiles(hid[:, 0], 2 + g, 0),
                       u_high, g + 1, u_ready)

            def taps(lo, hi):
                for n in range(lo, hi):
                    pair, step = divmod(n, 2 * TAPS)
                    tap, i = divmod(step, 2)
                    t = 2 * pair + i
                    w = par[:, C_CONV + t * TAPS + tap:C_CONV + t * TAPS + tap + 1]
                    src = conv_in[:, t, FROM1 + tap:FROM1 + tap + N1]
                    if tap == 0:
                        dve.wait_ge(glu_ready, pair + 1)
                        dve.tensor_scalar(conv[:, t, FROM1:], src, w, par[:, C_BIAS + t:C_BIAS + t + 1],
                                          ALU.mult, ALU.add).then_inc(tap_done, 1)
                    else:
                        dve.wait_ge(tap_done, n - 1)
                        dve.scalar_tensor_tensor(conv[:, t, FROM1:], src, w, conv[:, t, FROM1:],
                                                 ALU.mult, ALU.add).then_inc(tap_done, 1)

            def split_v(hd):
                low_of(vs[0:TOK, hd % 2, 1, :, :], banks[0:TOK, ch_bank(hd):ch_bank(hd) + 3, :],
                       vs[0:TOK, hd % 2, 0, :, :], v_high, hd + 1, v_ready)

            def split_ya(hd):
                low_of(hid[:, 1, 2 * hd:2 * hd + 2, FROM1:], seq_psum(hd),
                       hid[:, 0, 2 * hd:2 * hd + 2, FROM1:], ya_high, hd + 1, ya_ready)

            def head_tiles(hd):
                return conv[:, 2 * hd:2 * hd + 2, FROM1:]

            def ln_centre(hd, bank):
                dve.wait_ge(ln_mean, hd + 1)
                mean = banks[:, bank, 0:N1].unsqueeze(1).broadcast_to([P, 2, N1])
                dve.scalar_tensor_tensor(head_tiles(hd), mean, -1.0 / HEAD_DIM, head_tiles(hd),
                                         ALU.mult, ALU.add).then_inc(ln_centred, 1)

            def ln_norm(hd):
                dve.wait_ge(ln_root, hd + 1)
                dve.reciprocal(act4[:, hd, FROM1:], act4[:, hd, FROM1:]).then_inc(ln_rstd, 1)
                dve.wait_ge(ln_rstd, hd + 1)
                dve.tensor_tensor(head_tiles(hd), head_tiles(hd), over(act4[:, hd], 2, FROM1),
                                  ALU.mult).then_inc(ln_normed, 1)

            def ln_silu(hd):
                dve.wait_ge(ln_affine, 2 * hd + 2)
                dve.tensor_tensor(head_tiles(hd), head_tiles(hd), sq4[:, 2 * (hd % 2):2 * (hd % 2) + 2, FROM1:],
                                  ALU.mult).then_inc(ln_out, 1)

            def split_yb(hd):
                tiles_ = slice(KT // 2 + 2 * hd, KT // 2 + 2 * hd + 2)
                low_of(hid[:, 1, tiles_, FROM1:], head_tiles(hd), hid[:, 0, tiles_, FROM1:],
                       yb_high, hd + 1, yb_ready)

            E = RING

            dve.wait_ge(par_landed, 16)
            for q in range(KT // M):
                split_x(0, q, 0)
                slabs(0, q, q + 1)
            dve.wait_ge(table_high, 1)
            dve.tensor_tensor(tch[:, 1, :], raw_ch, tch[:, 0, :].bitcast(F32),
                              ALU.subtract).then_inc(table_ready, 1)
            dve.wait_ge(table_high, 2)
            dve.tensor_tensor(tseq[:, 1, :], raw_seq, tseq[:, 0, :].bitcast(F32),
                              ALU.subtract).then_inc(table_ready, 1)
            dve.wait_ge(consts_set, 4)
            slabs(0, E, SLABS)
            reciprocal(0, 0)

            tap = 0
            PER_SLAB = 4
            for g in range(1, 6):
                for j in range(SLABS):
                    slabs(SLABS * g, j, j + 1)
                    if j == E - 1:
                        glu(g - 1, SLABS * g) if g < 5 else split_u(0, SLABS * g)
                    elif g > 1 or j >= E:
                        n = min(PER_SLAB, 2 * TAPS * min(g, 4) - tap)
                        taps(tap, tap + n)
                        tap += n
            split_u(1, S_OUT_A)
            slabs(S_OUT_A, 0, RING)

            def more_taps(n):
                nonlocal tap
                n = min(n, CONV_TILES * TAPS - tap)
                taps(tap, tap + n)
                tap += n

            split_v(0)
            split_v(1)
            more_taps(10)
            split_ya(0)
            more_taps(10)
            split_v(2)
            more_taps(10)
            split_ya(1)
            more_taps(10)
            split_v(3)
            more_taps(10)
            split_ya(2)
            more_taps(10)
            split_ya(3)
            slabs(S_OUT_A, 4, 5)
            more_taps(2)
            slabs(S_OUT_A, 5, 6)
            for hd in range(3):
                ln_centre(hd, M + hd)
            slabs(S_OUT_A, 6, 7)
            more_taps(6)
            slabs(S_OUT_A, 7, 8)
            residual(0, S_OUT_A + 4, G_OUT_A, 0, FROM1)
            more_taps(6)
            slabs(S_OUT_A, 8, 9)
            more_taps(6)
            slabs(S_OUT_A, 9, 10)
            more_taps(CONV_TILES * TAPS)
            slabs(S_OUT_A, 10, 11)
            ln_centre(3, 3)
            slabs(S_OUT_A, 11, 12)
            residual(1, S_OUT_A + 8, G_OUT_A + 1, 1, FROM1)
            for hd in range(3):
                ln_norm(hd)
            slabs(S_OUT_A, 12, 14)
            ln_norm(3)
            slabs(S_OUT_A, 14, 16)
            residual(2, S_OUT_A + 12, G_OUT_A + 2, 0, FROM1)
            for hd in range(HEADS):
                ln_silu(hd)
                split_yb(hd)
                if hd:
                    slabs(S_OUT_B, hd - 1, hd)
            slabs(S_OUT_B, 3, 4)
            residual(3, S_OUT_B, G_OUT_A + 3, 1, FROM1)
            slabs(S_OUT_B, 4, 8)
            for g in range(3):
                residual(g, S_OUT_B + 4 * g + 4, G_OUT_B + g, g % 2, FROM1)
                split_x(1, g, FROM1)
                if g < 2:
                    slabs(S_OUT_B, 8 + 4 * g, 12 + 4 * g)

            def mlp(slab0, norm, lo, index0, r0, next_norm, next_lo, prev_lo):
                def quarter(q, first=False, last=False):
                    s0, r, i0 = q * SQ + slab0, q * 4 + r0, q * GQ + index0
                    for g in range(GQ):
                        slabs(s0, SLABS * g, SLABS * g + E)
                        end, index, parity = s0 + SLABS * g, i0 + (g - 1), (g - 1) % 2
                        if g == 0:
                            residual(3, end, index, parity, prev_lo if first else lo)
                            if first:
                                split_x(norm, 3, lo)
                        elif g <= 4:
                            relu_split(r + (g - 1), g - 1, end, index, parity, lo)
                        else:
                            residual(g - 5, end, index, parity, lo)
                            if last and next_norm < 4:
                                split_x(next_norm, g - 5, next_lo)
                        slabs(s0, SLABS * g + E, SLABS * g + SLABS)
                        if g == 0 and first:
                            reciprocal(norm, lo)
                quarter(0, first=True)
                with dve.Fori(1, QUARTERS - 1) as q:
                    quarter(q)
                quarter(QUARTERS - 1, last=True)

            mlp(S_MLP0, 1, FROM1, G_MLP0, 0, 2, FROM1, FROM1)

            def gated(j, slab_end, index):
                scale(act4[:, :, FROM1:], slab_end, index, FROM1)
                for tap_ in range(3):
                    for i in range(M):
                        c = C_SHORT + (M * j + i) * 3 + tap_
                        n = 3 * M * j + M * tap_ + i
                        dst, src = short_out[:, i, :], short_in[:, i, tap_ + 1:tap_ + 1 + N2]
                        if tap_ == 0:
                            dve.tensor_scalar(dst, src, par[:, c:c + 1], None, ALU.mult).then_inc(short_tap, 1)
                        else:
                            dve.wait_ge(short_tap, n - M + 1)
                            dve.scalar_tensor_tensor(dst, src, par[:, c:c + 1], dst, ALU.mult,
                                                     ALU.add).then_inc(short_tap, 1)
                dve.wait_ge(short_tap, 3 * M * (j + 1))
                dve.tensor_tensor(short_out, short_out, act4[:, :, FROM2:], ALU.mult).then_inc(y_ready, 1)
                low_of(tiles(hid[:, 1], j, FROM2), short_out, tiles(hid[:, 0], j, FROM2),
                       y_high, j + 1, gated_ready)

            for i in range(4):
                for k in range(3):
                    s0, index = S_C_IN + SLABS * (3 * i + k), G_C_IN + 3 * i + k - 1
                    slabs(s0, 0, E)
                    if k == 0 and i == 0:
                        residual(3, s0, index, index % 2, FROM1)
                        split_x(2, 3, FROM1)
                        dve.memset(conv_in[:, 0:M, N1:N1 + 1], 0.0).then_inc(consts_set, 1)
                        dve.wait_ge(consts_set, 5)
                    elif k == 0:
                        gated(i - 1, s0, index)
                    elif k == 1:
                        scale(gate_c, s0, index, FROM1)
                    else:
                        scale(act4[:, :, FROM1:], s0, index, FROM1)
                        dve.wait_ge(banks_free, index + 1)
                        dve.tensor_tensor(short_in[:, :, 0:N1], act4[:, :, FROM1:], gate_c,
                                          ALU.mult).then_inc(short_ready, 1)
                        dve.wait_ge(short_ready, i + 1)
                    slabs(s0, E, SLABS)
                    if k == 0 and i == 0:
                        reciprocal(2, FROM1)
            for g in range(4):
                s0 = S_C_OUT + SLABS * g
                slabs(s0, 0, E)
                if g == 0:
                    gated(3, s0, G_C_OUT - 1)
                else:
                    residual(g - 1, s0, G_C_OUT + g - 1, (g - 1) % 2, FROM2)
                    split_x(3, g - 1, FROM2)
                slabs(s0, E, SLABS)

            mlp(S_MLP1, 3, FROM2, G_MLP1, 4 * QUARTERS, 4, FROM2, FROM2)
            residual(3, S_END, G_END - 1, 1, FROM2)
            reciprocal(4, FROM2)
            for g in range(4):
                dve.wait_ge(scaled, M * g + M)
                dve.tensor_tensor(tiles(h, g, FROM2), tiles(h, g, FROM2), over(rstd, M, FROM2),
                                  ALU.mult).then_inc(normed, 1)


def dft_tables():
    c = np.arange(HEAD_DIM)
    angle = 2 * np.pi * (np.outer(c, c) % HEAD_DIM) / HEAD_DIM
    ch = np.concatenate([np.cos(angle), np.sin(angle)], 1) / np.sqrt(HEAD_DIM)
    ch = ch.reshape(2, P, 2 * HEAD_DIM).transpose(1, 0, 2).reshape(P, 4 * HEAD_DIM)
    t = np.arange(L)
    angle = 2 * np.pi * (np.outer(t, t) % L) / L
    seq = np.concatenate([np.cos(angle), -np.sin(angle)], 1) / np.sqrt(L)
    parts = []
    for n, at in enumerate(TOK_AT):
        part = seq[at:at + TOK].copy()
        if n == 2:
            part[:TOK_AT[1] + TOK - at] = 0.0
        parts.append(part)
    return ch.astype(np.float32), np.concatenate(parts, 1).astype(np.float32)


def chunked(w, k0, k1, cols):
    part = np.concatenate([w[k0:k1, a:b] for a, b in cols], 1)
    n = (k1 - k0) // (P * CHUNK_K)
    return part.reshape(n, CHUNK_K, P, COLS).transpose(0, 2, 1, 3).reshape(n, P, CHUNK_K * COLS)


def weight_chunks(ab_w_in, ab_w_out, c_w_in, c_w_out, mlp_w1, mlp_w2):
    def span(n, at=0):
        return [(at + COLS * n, at + COLS * n + COLS)]

    def mlp(w1, w2):
        for q in range(QUARTERS):
            for g in range(4):
                yield chunked(w1, 0, D, span(g, D * q))
            for g in range(4):
                yield chunked(w2, D * q, D * q + D, span(g))

    half = D // 2
    out = []
    for g in range(4):
        a, b = half + COLS // 2 * g, 2 * half + COLS // 2 * g
        out.append(chunked(ab_w_in[0], 0, D, [(a, a + COLS // 2), (b, b + COLS // 2)]))
    for g in range(2):
        out.append(chunked(ab_w_in[0], 0, D, span(g)))
    for k in range(2):
        for g in range(4):
            out.append(chunked(ab_w_out[0], half * k, half * k + half, span(g)))
    out += mlp(mlp_w1[0], mlp_w2[0])
    for j in range(4):
        out += [chunked(c_w_in[0], 0, D, span(j, at)) for at in (D, 2 * D, 0)]
    for g in range(4):
        out.append(chunked(c_w_out[0], 0, D, span(g)))
    out += mlp(mlp_w1[1], mlp_w2[1])
    return np.concatenate(out)


def packed_params(norms, conv_w, conv_b, ln_g, ln_b, short_w):
    cols = [n.reshape(KT, P).T for n in norms]
    cols.append(conv_w.reshape(TAPS, CONV_TILES, P).transpose(2, 1, 0).reshape(P, -1))
    cols += [v.reshape(CONV_TILES, P).T for v in (conv_b, ln_g, ln_b)]
    cols.append(short_w.reshape(3, KT, P).transpose(2, 1, 0).reshape(P, -1))
    return np.concatenate(cols, 1)


def kernel(**inputs):
    import concourse.bacc as bacc
    from concourse.bass_utils import run_bass_kernel_spmd

    a = {k: np.asarray(v) for k, v in inputs.items()}
    tokens = np.concatenate([a["meta_tokens"], a["x"][0]], 0)
    ch, seq = dft_tables()
    arrays = {
        "weights": weight_chunks(a["ab_w_in"], a["ab_w_out"], a["c_w_in"], a["c_w_out"],
                                 a["mlp_w1"], a["mlp_w2"]),
        "x": np.ascontiguousarray(tokens.T.reshape(KT, P, L).transpose(1, 0, 2)),
        "params": packed_params([a["norm_mix_g"][0], a["norm_mlp_g"][0], a["norm_mix_g"][1],
                                 a["norm_mlp_g"][1], a["norm_final_g"]], a["ab_conv_w"][0],
                                a["ab_conv_b"][0], a["ab_ln_g"][0], a["ab_ln_b"][0], a["c_conv_w"][0]),
        "dft_ch": ch,
        "dft_seq": seq,
    }
    nc = bacc.Bacc("TRN2", target_bir_lowering=False, num_devices=1)
    aps = {n: nc.dram_tensor(n, v.shape, F32, kind="ExternalInput").ap() for n, v in arrays.items()}
    out = nc.dram_tensor("out", (P, KT, SEQ), F32, kind="ExternalOutput").ap()
    trunk(nc, aps["weights"], aps["x"], aps["params"], aps["dft_ch"], aps["dft_seq"], out)
    r = run_bass_kernel_spmd(nc, [arrays], core_ids=[0])
    y = r.results[0]["out"]
    return np.ascontiguousarray(y.transpose(1, 0, 2).reshape(D, SEQ).T)[None]
```

```python
from contextlib import ExitStack

import numpy as np
import concourse.bass as bass
from concourse import mybir

F32 = mybir.dt.float32
F32R = mybir.dt.float32r
ALU = mybir.AluOpType
ACT = mybir.ActivationFunctionType

P = 128
D = 2048
META, SEQ = 16, 256
L = META + SEQ
DFF = 4 * D
KT = D // P
HEADS, HEAD_DIM = 4, D // 8
TAPS, PAD = 31, 15
CONV_TILES = HEADS * HEAD_DIM // P
EPS = 1e-6

COLS = 512
M = COLS // P
CHUNK_K = 4
SLAB_K = 2
SLABS = KT // SLAB_K
RAW = 4
RING = 4

FROM1 = META - 2
FROM2 = META
N0, N1, N2 = L, L - FROM1, L - FROM2

G_IN, G_OUT_A, G_OUT_B, G_MLP0 = 0, 6, 10, 14
G_C_IN, G_C_OUT, G_MLP1, G_END = 46, 58, 62, 94
S_IN, S_OUT_A, S_OUT_B, S_MLP0 = 0, 48, 72, 80
S_C_IN, S_C_OUT, S_MLP1, S_END = 336, 432, 464, 720
CHUNKS = S_END // 2
QUARTERS = 4
GQ, SQ = 8, 64

C_GAIN = 0
C_CONV = C_GAIN + 5 * KT
C_BIAS = C_CONV + CONV_TILES * TAPS
C_LNG = C_BIAS + CONV_TILES
C_LNB = C_LNG + CONV_TILES
C_SHORT = C_LNB + CONV_TILES
C_END = C_SHORT + KT * 3

TOK = 96
HALF_DFT = HEAD_DIM // 2 + 1
TOK_AT = (0, TOK, L - TOK)


def trunk(nc, weights, x, params, dft_ch, dft_seq, out):
    with ExitStack() as ctx:
        def sb(name, shape, dt=F32):
            return ctx.enter_context(nc.sbuf_tensor(name, shape, dt))

        def sem(name):
            return ctx.enter_context(nc.semaphore(name))

        h = sb("h", [P, KT, L])
        xs = sb("xs", [P, 2 * KT * L], F32R)
        hid = sb("hid", [P, 2, KT, L], F32R)
        raw = sb("raw", [P, RAW, CHUNK_K * COLS])
        wh = sb("wh", [P, RING, SLAB_K, COLS], F32R)
        wl = sb("wl", [P, RING, SLAB_K, COLS], F32R)
        rstd = sb("rstd", [P, L])
        act4 = sb("act4", [P, M, L])
        sq4 = sb("sq4", [P, M, L])
        ssum = sb("ssum", [P, M, L])
        par = sb("par", [P, C_END])
        ones = sb("ones", [P, P])
        eps = sb("eps", [P, 1])
        warm = sb("warm", [P, 5])
        conv_in = sb("conv_in", [P, CONV_TILES, L + 2 * PAD])
        conv = sb("conv", [P, CONV_TILES, L])
        tch = sb("tch", [P, 2, 2, 2 * HALF_DFT], F32R)
        tseq = sb("tseq", [TOK, 2, 3, 3, N1], F32R)

        xs4 = xs[:, :].rearrange("p (s k l) -> p s k l", s=2, k=KT)
        vs = xs[:, 0:2 * 2 * 3 * 2 * HALF_DFT].rearrange("p (b s t c) -> p b s t c", b=2, s=2, t=3)
        raw_ch = act4[:, :, :].rearrange("p m l -> p (m l)")[:, 0:4 * HALF_DFT] \
            .rearrange("p (k c) -> p k c", k=2)
        raw_seq = conv[:, :, :].rearrange("p m l -> p (m l)")[0:TOK, 0:3 * 2 * N1] \
            .rearrange("p (t f l) -> p t f l", t=3, f=2)
        flat_conv = conv[:, :, :].rearrange("p m l -> p (m l)")
        gate_c = flat_conv[:, 0:M * N1].rearrange("p (m l) -> p m l", m=M)
        short_out = flat_conv[:, M * N1:M * (N1 + N2)].rearrange("p (m l) -> p m l", m=M)
        short_in = conv_in[:, 0:M, 0:N1 + 1]

        banks = ctx.enter_context(nc.psum_tensor("banks", [P, 2 * M, COLS], F32))

        raw_landed = [sem(f"raw_landed{i}") for i in range(RAW)]
        x_landed = [sem(f"x_landed{i}") for i in range(KT // M)]
        gains_landed = sem("gains_landed")
        par_landed = sem("par_landed")
        x_first = sem("x_first")
        first_landed = sem("first_landed")
        ch_landed = sem("ch_landed")
        seq_landed = sem("seq_landed")
        stored = sem("stored")
        consts_set = sem("consts_set")
        high_ready = sem("high_ready")
        low_ready = sem("low_ready")
        slab_used = sem("slab_used")
        banks_free = sem("banks_free")
        x_high = sem("x_high")
        x_ready = sem("x_ready")
        squared = sem("squared")
        summed = sem("summed")
        ssum_ready = sem("ssum_ready")
        total_ready = sem("total_ready")
        root_ready = sem("root_ready")
        low_half = sem("low_half")
        joined = sem("joined")
        halves = sem("halves")
        tail_added = sem("tail_added")
        tail_sq = sem("tail_sq")
        rstd_ready = sem("rstd_ready")
        glu_sig = sem("glu_sig")
        glu_ready = sem("glu_ready")
        u_high = sem("u_high")
        u_ready = sem("u_ready")
        table_high = sem("table_high")
        table_ready = sem("table_ready")
        ch_done = sem("ch_done")
        v_high = sem("v_high")
        v_ready = sem("v_ready")
        seq_done = sem("seq_done")
        ya_high = sem("ya_high")
        ya_ready = sem("ya_ready")
        tap0_done = sem("tap0_done")
        tap_done = sem("tap_done")
        ln_sum = sem("ln_sum")
        ln_mean = sem("ln_mean")
        ln_centred = sem("ln_centred")
        ln_sq = sem("ln_sq")
        ln_sqsum = sem("ln_sqsum")
        ln_var = sem("ln_var")
        ln_root = sem("ln_root")
        ln_rstd = sem("ln_rstd")
        ln_normed = sem("ln_normed")
        ln_out = sem("ln_out")
        yb_high = sem("yb_high")
        yb_ready = sem("yb_ready")
        relu_sq = sem("relu_sq")
        relu_high = sem("relu_high")
        hid_ready = sem("hid_ready")
        short_ready = sem("short_ready")
        short_tap = sem("short_tap")
        y_ready = sem("y_ready")
        y_high = sem("y_high")
        gated_ready = sem("gated_ready")
        scaled = sem("scaled")
        normed = sem("normed")

        block = ctx.enter_context(nc.Block())

        def psum(parity, n, at=0):
            return banks[:, M * parity:M * parity + M, at:at + n]

        def tiles(t, g, lo):
            return t[:, M * g:M * g + M, lo:L]

        def over(tok, n_tiles, lo=0):
            return tok[:, lo:L].unsqueeze(1).broadcast_to([P, n_tiles, L - lo])

        def ch_bank(hd):
            return 5 * (hd % 2)

        def seq_bank(hd):
            return 3 if hd < 3 else 5

        def seq_psum(hd):
            return banks[:, seq_bank(hd):seq_bank(hd) + 2, 0:N1]

        def gain(norm, tile):
            return par[:, C_GAIN + norm * KT + tile:C_GAIN + norm * KT + tile + 1]

        @block.sync
        def _(sp):
            def load_chunk(n, slot, refill):
                if refill:
                    sp.wait_ge(low_ready, (n - RAW + 1) * 2)
                src = weights[n, :, :] if isinstance(n, int) else weights[bass.ds(n, 1), :, :]
                if not isinstance(n, int):
                    src = src.rearrange("a p c -> p (a c)")
                sp.dma_start(raw[:, slot, :], src).then_inc(raw_landed[slot], 16)

            half = CHUNK_K * COLS // 2
            sp.dma_start(h[:, 0:2, :], x[:, 0:2, :]).then_inc(x_first, 16)
            sp.dma_start(raw[:, 0, 0:half], weights[0, :, 0:half]).then_inc(first_landed, 16)
            sp.dma_start(h[:, 2:M, :], x[:, 2:M, :]).then_inc(x_landed[0], 16)
            sp.dma_start(raw[:, 0, half:], weights[0, :, half:]).then_inc(raw_landed[0], 16)
            for n in range(1, RAW):
                sp.dma_start(h[:, M * n:M * n + M, :], x[:, M * n:M * n + M, :]).then_inc(x_landed[n], 16)
                load_chunk(n, n, False)
            with sp.Fori(1, CHUNKS // RAW) as r:
                for slot in range(RAW):
                    load_chunk(r * RAW + slot, slot, True)
            for n in range(KT // 2):
                sp.wait_ge(normed, 2 * n + 2)
                sp.dma_start(out[:, 2 * n:2 * n + 2, :], h[:, 2 * n:2 * n + 2, FROM2:]).then_inc(stored, 16)
            sp.wait_ge(stored, 16 * (KT // 2))

        @block.gpsimd
        def _(pool):
            pool.memset(eps[:, :], EPS).then_inc(consts_set, 1)
            pool.memset(ones[:, :], 1.0).then_inc(consts_set, 1)
            pool.memset(conv_in[:, :, 0:PAD], 0.0).then_inc(consts_set, 1)
            pool.memset(conv_in[:, :, PAD + L:], 0.0).then_inc(consts_set, 1)
            pool.wait_ge(x_landed[2], 16)
            pool.dma_start(par[:, C_CONV:], params[:, C_CONV:]).then_inc(par_landed, 16)
            pool.dma_start(raw_ch, dft_ch).then_inc(ch_landed, 16)
            pool.dma_start(raw_seq, dft_seq).then_inc(seq_landed, 16)

            def sum_squares(norm, lo, quarters=KT // M):
                per_norm = KT // M - 1
                for q in range(1, quarters if norm else 3):
                    pool.wait_ge(squared, norm * (KT // M) + q + 1)
                    if q > 1:
                        pool.wait_ge(summed, norm * per_norm + q - 1)
                    pool.tensor_tensor(ssum[:, :, lo:], ssum[:, :, lo:], sq4[:, :, lo:],
                                       ALU.add).then_inc(summed, 1)
                if norm == 0:
                    return
                pool.wait_ge(summed, norm * per_norm + quarters - 1)
                pool.tensor_tensor(ssum[:, 0:2, lo:], ssum[:, 0:2, lo:], ssum[:, 2:4, lo:],
                                   ALU.add).then_inc(ssum_ready, 1)
                pool.wait_ge(ssum_ready, 2 * norm + 1)
                pool.tensor_tensor(ssum[:, 0, lo:], ssum[:, 0, lo:], ssum[:, 1, lo:],
                                   ALU.add).then_inc(ssum_ready, 1)

            def fold(dst, src, wait, count, done):
                pool.wait_ge(wait, count)
                pool.tensor_tensor(dst, src[0], src[1], ALU.add).then_inc(done, 1)

            sum_squares(0, 0)
            pool.wait_ge(total_ready, 1)
            def head_sum(hd):
                fold(ssum[:, hd, FROM1:], [conv[:, 2 * hd + i, FROM1:] for i in range(2)],
                     tap_done, (hd + 1) * 2 * (TAPS - 1), ln_sum)

            def head_sqsum(hd):
                pool.wait_ge(ln_mean, hd + 1)
                fold(ssum[:, hd, FROM1:], [sq4[:, 2 * (hd % 2) + i, FROM1:] for i in range(2)],
                     ln_sq, hd + 1, ln_sqsum)

            head_sum(0)
            head_sum(1)
            head_sqsum(0)
            head_sqsum(1)
            for hd in (2, 3):
                head_sum(hd)
                head_sqsum(hd)
            pool.wait_ge(ln_var, HEADS)
            sum_squares(1, FROM1)
            sum_squares(2, FROM1)
            sum_squares(3, FROM2)
            sum_squares(4, FROM2, quarters=3)

        @block.tensor
        def _(pe):
            def product(dst, w, v, start, stop):
                pe.matmul(dst, w[0], v[0], start=start, stop=False)
                pe.matmul(dst, w[0], v[1], start=False, stop=False)
                return pe.matmul(dst, w[1], v[0], start=False, stop=stop)

            def wide_product(bank, w, v, start, stop):
                n = v[0].shape[-1]
                pe.matmul(bank[:, 0:2 * n].rearrange("p (s n) -> p s n", s=2), w[0], v[1],
                          start=start, stop=False)
                return pe.matmul(bank[:, 0:n], w[1], v[0], start=False, stop=stop)

            def group(slab0, index, parity, moving, lo, n_slabs=SLABS, tile0=0, ready=None, side=None,
                      ring0=0):
                if not isinstance(index, int) or index >= 2:
                    pe.wait_ge(banks_free, index - 1)
                for s in range(n_slabs):
                    pe.wait_ge(low_ready, slab0 + (s + 1))
                    if ready:
                        ready(s)
                    for m in range(M):
                        for t in range(SLAB_K):
                            k = tile0 + SLAB_K * s + t
                            slot = (ring0 + s) % RING
                            cols = slice(P * m, P * m + P)
                            w = wh[:, slot, t, cols], wl[:, slot, t, cols]
                            start, stop = s + t == 0, s == n_slabs - 1 and t == SLAB_K - 1
                            if 2 * (L - lo) <= COLS:
                                last = wide_product(banks[:, M * parity + m, :], w,
                                                    (moving[:, 0, k, lo:L], moving[:, :, k, lo:L]),
                                                    start, stop)
                            else:
                                last = product(banks[:, M * parity + m, 0:L - lo], w,
                                               (moving[:, 0, k, lo:L], moving[:, 1, k, lo:L]),
                                               start, stop)
                    last.then_inc(slab_used, 1)
                    if side and s in side:
                        side[s]()

            def x_tiles(norm):
                return lambda s: pe.wait_ge(x_ready, norm * SLABS + s + 1)

            def norm_total(norm, lo):
                def run():
                    pe.wait_ge(ssum_ready, 2 * norm + 2)
                    if norm:
                        pe.wait_ge(banks_free, (G_IN, G_MLP0, G_C_IN, G_MLP1)[norm])
                    pe.matmul(banks[:, M, 0:L - lo], ones[:, :], ssum[:, 0, lo:],
                              start=True, stop=True).then_inc(total_ready, 1)
                return run

            def final_total():
                pe.wait_ge(ssum_ready, 2 * 4 + 2)
                pe.wait_ge(banks_free, G_END - 1)
                pe.matmul(banks[:, 0, 0:N2], ones[:, :], ssum[:, 0, FROM2:], start=True, stop=False)
                for m in range(M):
                    pe.wait_ge(tail_sq, m + 1)
                    last = pe.matmul(banks[:, 0, 0:N2], ones[:, :], sq4[:, m, FROM2:],
                                     start=False, stop=m == M - 1)
                last.then_inc(total_ready, 1)

            def x_phase(slab0, index0, pairs, norm, lo):
                group(slab0, index0, 0, xs4, lo, ready=x_tiles(norm), side={6: norm_total(norm, lo)})
                pe.wait_ge(root_ready, norm + 1)
                group(slab0 + SLABS, index0 + 1, 1, xs4, lo)
                if pairs > 1:
                    with pe.Fori(1, pairs) as i:
                        for par_ in range(2):
                            group(i * (2 * SLABS) + (slab0 + SLABS * par_), i * 2 + (index0 + par_),
                                  par_, xs4, lo)

            def hid_phase(slab0, index0, pairs, lo, ready):
                with pe.Fori(0, pairs) as i:
                    for par_ in range(2):
                        group(i * (2 * SLABS) + (slab0 + SLABS * par_), i * 2 + (index0 + par_),
                              par_, hid, lo, ready=ready)

            def mlp(slab0, index0, norm, lo, hid0):
                x_phase(slab0, index0, 2, norm, lo)
                hid_phase(slab0 + SQ // 2, index0 + GQ // 2, 2, lo,
                          lambda s: s % 2 == 0 and pe.wait_ge(hid_ready, hid0 + s // 2 + 1))
                with pe.Fori(1, QUARTERS) as q:
                    with pe.Fori(0, 2) as i:
                        for par_ in range(2):
                            group(q * SQ + i * (2 * SLABS) + (slab0 + SLABS * par_),
                                  q * GQ + i * 2 + (index0 + par_), par_, xs4, lo)
                    with pe.Fori(0, 2) as i:
                        for par_ in range(2):
                            group(q * SQ + i * (2 * SLABS) + (slab0 + SQ // 2 + SLABS * par_),
                                  q * GQ + i * 2 + (index0 + GQ // 2 + par_), par_, hid, lo,
                                  ready=lambda s: s % 2 == 0 and pe.wait_ge(
                                      hid_ready, q * 4 + (hid0 + s // 2 + 1)))

            def channel_dft(hd):
                pe.wait_ge(u_ready, hd // 2 + 1)
                if hd == 0:
                    pe.wait_ge(ln_centred, 2)
                if hd == 1:
                    pe.wait_ge(banks_free, G_OUT_A)
                for t, at in enumerate(TOK_AT):
                    for k in range(2):
                        u = hid[:, :, KT // 2 + 2 * hd + k, at:at + TOK]
                        last = product(banks[0:TOK, ch_bank(hd) + t, 0:2 * HALF_DFT], (u[:, 0], u[:, 1]),
                                       (tch[:, 0, k, :], tch[:, 1, k, :]), k == 0, k == 1)
                last.then_inc(ch_done, 1)

            def sequence_dft(hd):
                pe.wait_ge(v_ready, hd + 1)
                if hd == 0:
                    pe.wait_ge(ln_root, 2)
                elif hd < 3:
                    pe.wait_ge(ya_ready, hd)
                for j in range(2):
                    for f in range(2):
                        for t in range(3):
                            cols = slice(HALF_DFT * f + j, HALF_DFT * f + j + P)
                            v = vs[0:TOK, hd % 2, :, t, cols]
                            table = tseq[:, :, t, f + (f & j), :]
                            last = product(banks[:, seq_bank(hd) + j, 0:N1], (v[:, 0], v[:, 1]),
                                           (table[:, 0], table[:, 1]), f + t == 0, f == 1 and t == 2)
                last.then_inc(seq_done, 1)

            def ln_total(hd, bank, ready, done):
                pe.wait_ge(ready, hd + 1)
                pe.matmul(banks[:, bank, 0:N1], ones[:, :], ssum[:, hd, FROM1:],
                          start=True, stop=True).then_inc(done, 1)

            def ln_totals(heads, free, bank, ready, done):
                def run():
                    if free:
                        pe.wait_ge(banks_free, free)
                    for n, hd in enumerate(heads):
                        ln_total(hd, bank + n, ready, done)
                return run

            pe.wait_ge(consts_set, 4)
            x_phase(S_IN, G_IN, 2, 0, 0)
            group(S_IN + 4 * SLABS, G_IN + 4, 0, xs4, 0)
            group(S_IN + 5 * SLABS, G_IN + 5, 1, xs4, 0,
                  side={5: ln_totals((0, 1), G_IN + 5, 0, ln_sum, ln_mean)})

            pe.wait_ge(table_ready, 3)
            channel_dft(0)
            ln_totals((0, 1), G_OUT_A, 3, ln_sqsum, ln_var)()
            channel_dft(1)
            sequence_dft(0)
            channel_dft(2)
            sequence_dft(1)
            channel_dft(3)
            sequence_dft(2)
            sequence_dft(3)

            n_a, n_b = (S_OUT_B - S_OUT_A) // 4, (S_MLP0 - S_OUT_B) // 4
            sides = [None,
                     None,
                     {1: ln_totals((2,), G_OUT_A + 2, M, ln_sum, ln_mean),
                      4: ln_totals((2,), None, M + 1, ln_sqsum, ln_var)},
                     {2: ln_totals((3,), G_OUT_A + 3, 0, ln_sum, ln_mean),
                      3: ln_totals((3,), None, 1, ln_sqsum, ln_var)}]

            def mixed(s):
                if s < HEADS:
                    pe.wait_ge(ya_ready, s + 1)
                else:
                    pe.wait_ge(yb_ready, s - HEADS + 1)

            pe.wait_ge(ya_ready, 3)
            for g in range(4):
                if g == 3:
                    pe.wait_ge(ln_root, 3)
                group(S_OUT_A + n_a * g, G_OUT_A + g, g % 2, hid, FROM1, n_slabs=n_a,
                      ready=mixed if g == 0 else None, side=sides[g], ring0=n_a * g)
            pe.wait_ge(ln_root, 4)
            for g in range(4):
                group(S_OUT_B + n_b * g, G_OUT_B + g, g % 2, hid, FROM1, n_slabs=n_b,
                      tile0=SLAB_K * n_a, ready=(lambda s: pe.wait_ge(yb_ready, s + 3)) if g == 0 else None,
                      ring0=n_b * g)

            mlp(S_MLP0, G_MLP0, 1, FROM1, 0)

            x_phase(S_C_IN, G_C_IN, 6, 2, FROM1)
            hid_phase(S_C_OUT, G_C_OUT, 2, FROM2,
                      lambda s: s % 2 == 0 and pe.wait_ge(gated_ready, s // 2 + 1))
            mlp(S_MLP1, G_MLP1, 3, FROM2, QUARTERS * 4)
            final_total()

        @block.scalar
        def _(act):
            def high(slab0, j):
                slab, chunk_slot = slab0 + j, (j // 2) % RAW
                if isinstance(slab, int) and slab == 0:
                    act.wait_ge(first_landed, 16)
                elif j % 2 == 0 or isinstance(slab, int) and slab == 1:
                    loads = j // (2 * RAW) + 1
                    act.wait_ge(raw_landed[chunk_slot], slab0 * (16 // (2 * RAW)) + 16 * loads)
                if not isinstance(slab, int) or slab >= RING:
                    act.wait_ge(slab_used, slab - (RING - 1))
                src = raw[:, chunk_slot, SLAB_K * COLS * (j % 2):SLAB_K * COLS * (j % 2 + 1)]
                act.activation(wh[:, j % RING, :, :], src.rearrange("p (t c) -> p t c", t=SLAB_K),
                               ACT.Copy).then_inc(high_ready, 1)

            def slabs(slab0, lo, hi):
                for j in range(lo, hi):
                    high(slab0, j)

            def split_x(norm, g, lo, residual=None):
                if residual is not None:
                    act.wait_ge(banks_free, residual)
                gained(norm, g, lo)
                square(norm, g, lo)

            def gained(norm, g, lo, first=0, end=M):
                for t in range(M * g + first, M * g + end):
                    act.activation(xs4[:, 0, t, lo:], h[:, t, lo:], ACT.Copy,
                                   scale=gain(norm, t)).then_inc(x_high, 1)

            def square(norm, g, lo):
                if g == 0 and norm:
                    act.wait_ge(total_ready, norm)
                if g > 1:
                    act.wait_ge(summed, norm * (KT // M - 1) + g - 1)
                dst = ssum if g == 0 else sq4
                act.activation(dst[:, :, lo:], tiles(h, g, lo), ACT.Square).then_inc(squared, 1)

            def norm_root(norm, lo):
                act.wait_ge(total_ready, norm + 1)
                bank = M if norm < 4 else 0
                act.activation(rstd[:, lo:], banks[:, bank, 0:L - lo], ACT.Sqrt,
                               bias=eps[:, :], scale=1.0 / D).then_inc(root_ready, 1)

            def relu_split(r, slab_end, index, parity, g, lo):
                if lo == FROM2:
                    act.wait_ge(slab_used, slab_end)
                    act.activation(act4[:, :, lo:], psum(parity, N2, N2), ACT.Copy).then_inc(low_half, 1)
                    act.wait_ge(joined, r - 4 * QUARTERS + 1)
                else:
                    act.wait_ge(banks_free, index + 1)
                act.activation(sq4[:, :, lo:], act4[:, :, lo:], ACT.Square).then_inc(relu_sq, 1)
                act.wait_ge(relu_sq, r + 1)
                act.activation(tiles(hid[:, 0], g, lo), sq4[:, :, lo:], ACT.Copy).then_inc(relu_high, 1)

            def glu(g):
                act.wait_ge(banks_free, g + 1)
                act.activation(sq4[:, 0:2, :], act4[:, 2:4, :], ACT.Sigmoid).then_inc(glu_sig, 1)

            def split_channel_table():
                act.wait_ge(ch_landed, 16)
                act.activation(tch[:, 0, :, :], raw_ch, ACT.Copy).then_inc(table_high, 1)

            def split_sequence_table():
                act.wait_ge(seq_landed, 16)
                act.activation(tseq[:, 0, :, 0:2, :], raw_seq, ACT.Copy).then_inc(table_high, 1)
                act.activation(tseq[:, 0, :, 2, :], raw_seq[:, :, 1, :], ACT.Copy, scale=-1.0).then_inc(table_high, 1)

            def first_taps(pair):
                act.wait_ge(glu_ready, pair + 1)
                if pair == 0:
                    act.wait_ge(table_ready, 3)
                for t in (2 * pair, 2 * pair + 1):
                    act.activation(conv[:, t, FROM1:], conv_in[:, t, FROM1:FROM1 + N1], ACT.Identity,
                                   bias=par[:, C_BIAS + t:C_BIAS + t + 1],
                                   scale=par[:, C_CONV + t * TAPS:C_CONV + t * TAPS + 1]).then_inc(tap0_done, 1)

            def split_u(g):
                act.wait_ge(banks_free, 5 + g)
                act.activation(tiles(hid[:, 0], 2 + g, 0), act4[:, :, :], ACT.Copy).then_inc(u_high, 1)

            def split_v(hd):
                act.wait_ge(ch_done, hd + 1)
                act.activation(vs[0:TOK, hd % 2, 0, :, :], banks[0:TOK, ch_bank(hd):ch_bank(hd) + 3, 0:2 * HALF_DFT],
                               ACT.Copy).then_inc(v_high, 1)

            def split_ya(hd):
                act.wait_ge(seq_done, hd + 1)
                act.activation(hid[:, 0, 2 * hd:2 * hd + 2, FROM1:], seq_psum(hd), ACT.Copy).then_inc(ya_high, 1)

            def head_tiles(hd):
                return conv[:, 2 * hd:2 * hd + 2, FROM1:]

            def ln_square(hd):
                act.wait_ge(ln_centred, hd + 1)
                if hd >= 2:
                    act.wait_ge(ln_sqsum, hd - 1)
                act.activation(sq4[:, 2 * (hd % 2):2 * (hd % 2) + 2, FROM1:], head_tiles(hd),
                               ACT.Square).then_inc(ln_sq, 1)

            def ln_roots(hd, bank):
                act.wait_ge(ln_var, hd + 1)
                act.activation(ssum[:, hd, FROM1:], banks[:, bank, 0:N1], ACT.Sqrt,
                               bias=eps[:, :], scale=1.0 / HEAD_DIM).then_inc(ln_root, 1)

            def ln_silu(hd):
                act.wait_ge(ln_normed, hd + 1)
                for t in (2 * hd, 2 * hd + 1):
                    act.activation(conv[:, t, FROM1:], conv[:, t, FROM1:], ACT.Silu,
                                   bias=par[:, C_LNB + t:C_LNB + t + 1],
                                   scale=par[:, C_LNG + t:C_LNG + t + 1]).then_inc(ln_out, 1)

            def split_yb(hd):
                act.wait_ge(ln_out, 2 * hd + 2)
                act.activation(hid[:, 0, KT // 2 + 2 * hd:KT // 2 + 2 * hd + 2, FROM1:], head_tiles(hd),
                               ACT.Copy).then_inc(yb_high, 1)

            def split_gated(j):
                act.wait_ge(y_ready, j + 1)
                act.activation(tiles(hid[:, 0], j, FROM2), short_out, ACT.Copy).then_inc(y_high, 1)

            E = RING
            EARLY = 2

            act.dma_start(par[:, :C_CONV], params[:, :C_CONV]).then_inc(gains_landed, 16)
            act.wait_ge(consts_set, 1)
            act.activation(warm[:, 0:1], eps[:, :], ACT.Sqrt)
            act.wait_ge(gains_landed, 16)
            act.wait_ge(x_first, 16)
            gained(0, 0, 0, 0, 2)
            slabs(0, 0, 1)
            act.wait_ge(x_landed[0], 16)
            gained(0, 0, 0, 2, M)
            slabs(0, 1, 2)
            square(0, 0, 0)
            for q in range(1, KT // M):
                act.wait_ge(x_landed[q], 16)
                gained(0, q, 0)
                slabs(0, 2 * q, 2 * q + 2)
                square(0, q, 0)
            split_channel_table()
            slabs(SLABS, 0, EARLY)
            split_sequence_table()
            norm_root(0, 0)
            act.wait_ge(par_landed, 16)
            for g in range(1, 6):
                slabs(SLABS * g, EARLY if g == 1 else 0, E)
                glu(g - 1) if g < 5 else split_u(0)
                slabs(SLABS * g, E, E + 1)
                if g < 5:
                    first_taps(g - 1)
                slabs(SLABS * g, E + 1, SLABS)
            ln_square(0)
            ln_square(1)
            act.activation(warm[:, 1:2], eps[:, :], ACT.Sqrt)
            split_u(1)
            split_v(0)
            ln_roots(0, 3)
            ln_roots(1, 4)
            act.activation(warm[:, 2:3], eps[:, :], ACT.Silu)
            split_v(1)
            slabs(S_OUT_A, 0, 2)
            split_ya(0)
            split_v(2)
            ln_silu(0)
            split_ya(1)
            split_v(3)
            split_yb(0)
            ln_silu(1)
            slabs(S_OUT_A, 2, RING)
            split_ya(2)
            split_yb(1)
            split_ya(3)
            slabs(S_OUT_A, 4, 18)
            ln_square(2)
            slabs(S_OUT_A, 18, 19)
            act.activation(warm[:, 3:4], eps[:, :], ACT.Sqrt)
            slabs(S_OUT_A, 19, 20)
            ln_roots(2, M + 1)
            slabs(S_OUT_A, 20, 24)
            ln_square(3)
            slabs(S_OUT_A, 24, 25)
            ln_roots(3, 1)
            act.activation(warm[:, 4:5], eps[:, :], ACT.Silu)
            ln_silu(2)
            ln_silu(3)
            split_yb(2)
            slabs(S_OUT_A, 25, 26)
            split_yb(3)
            slabs(S_OUT_A, 26, 30)
            split_x(1, 0, FROM1, G_OUT_B + 1)
            slabs(S_OUT_A, 30, 32)
            split_x(1, 1, FROM1, G_OUT_B + 2)

            def mlp(slab0, norm, lo, index0, r0, next_norm, next_lo):
                def quarter(q, first=False, last=False):
                    s0, r = q * SQ + slab0, q * 4 + r0
                    for g in range(GQ):
                        if g == 0 and first and norm == 1:
                            slabs(s0, 0, 2)
                            split_x(norm, 2, lo, index0 - 1)
                            slabs(s0, 2, E)
                        else:
                            slabs(s0, SLABS * g + (EARLY if g == 1 and first else 0), SLABS * g + E)
                        if g == 0 and first:
                            split_x(norm, 3, lo, index0)
                        if 1 <= g <= 4:
                            relu_split(r + (g - 1), s0 + SLABS * g, q * GQ + (index0 + g - 1),
                                       (g - 1) % 2, g - 1, lo)
                        if g > 4 and last:
                            if next_norm < 4:
                                split_x(next_norm, g - 5, next_lo, index0 + 3 * GQ + g)
                            else:
                                act.wait_ge(banks_free, index0 + 3 * GQ + g)
                                square(4, g - 5, next_lo)
                                act.wait_ge(squared, 4 * (KT // M) + g - 4)
                                for t in range(M * (g - 5), M * (g - 4)):
                                    act.activation(h[:, t, next_lo:], h[:, t, next_lo:], ACT.Copy,
                                                   scale=gain(4, t)).then_inc(scaled, 1)
                        slabs(s0, SLABS * g + E, SLABS * g + SLABS)
                        if g == 0 and first:
                            slabs(s0, SLABS, SLABS + EARLY)
                            norm_root(norm, lo)
                quarter(0, first=True)
                with act.Fori(1, QUARTERS - 1) as q:
                    quarter(q)
                quarter(QUARTERS - 1, last=True)

            mlp(S_MLP0, 1, FROM1, G_MLP0, 0, 2, FROM1)

            def gated_three(i, first=False):
                for k in range(3):
                    s0 = i * (3 * SLABS) + (S_C_IN + SLABS * k)
                    slabs(s0, EARLY if k == 1 and first else 0, E)
                    if k == 0:
                        if first:
                            split_x(2, 3, FROM1, G_C_IN)
                        else:
                            split_gated_at(i - 1)
                    slabs(s0, E, SLABS)
                    if k == 0 and first:
                        slabs(s0, SLABS, SLABS + EARLY)
                        norm_root(2, FROM1)

            def split_gated_at(j):
                split_gated(j)

            for i in range(4):
                gated_three(i, first=(i == 0))
            for g in range(4):
                slabs(S_C_OUT + SLABS * g, 0, E)
                if g == 0:
                    split_gated(3)
                else:
                    split_x(3, g - 1, FROM2, G_C_OUT + g)
                slabs(S_C_OUT + SLABS * g, E, SLABS)

            mlp(S_MLP1, 3, FROM2, G_MLP1, 4 * QUARTERS, 4, FROM2)
            for m in range(M):
                if m == 0:
                    act.wait_ge(summed, 4 * (KT // M - 1) + 2)
                act.wait_ge(joined, 4 * QUARTERS + m // 2 + 1)
                act.activation(sq4[:, m, FROM2:], h[:, KT - M + m, FROM2:], ACT.Square).then_inc(tail_sq, 1)
            norm_root(4, FROM2)

        @block.vector
        def _(dve):
            def low(slab, j):
                dve.wait_ge(high_ready, slab + 1)
                src = raw[:, (j // 2) % RAW, SLAB_K * COLS * (j % 2):SLAB_K * COLS * (j % 2 + 1)]
                dve.tensor_tensor(wl[:, j % RING, :, :], src.rearrange("p (t c) -> p t c", t=SLAB_K),
                                  wh[:, j % RING, :, :].bitcast(F32), ALU.subtract).then_inc(low_ready, 1)

            def slabs(slab0, lo, hi):
                for j in range(lo, hi):
                    low(slab0 + j, j)

            def split_x(norm, g, lo, first=0, end=M):
                for t in range(M * g + first, M * g + end):
                    dve.wait_ge(x_high, norm * KT + t + 1)
                    last = dve.scalar_tensor_tensor(xs4[:, 1, t, lo:], h[:, t, lo:], gain(norm, t),
                                                    xs4[:, 0, t, lo:].bitcast(F32), ALU.mult, ALU.subtract)
                    if t % 2 == 1:
                        last.then_inc(x_ready, 1)

            def group_done(slab_end, index):
                dve.wait_ge(slab_used, slab_end)
                if not isinstance(index, int) or index > 0:
                    dve.wait_ge(banks_free, index)

            def residual(g, slab_end, index, parity, lo, nth=None):
                group_done(slab_end, index)
                if lo == FROM2:
                    dve.tensor_tensor(tiles(h, g, lo), tiles(h, g, lo), psum(parity, N2, N2),
                                      ALU.add).then_inc(halves, 1)
                    dve.wait_ge(halves, nth + 1)
                dve.tensor_tensor(tiles(h, g, lo), tiles(h, g, lo), psum(parity, L - lo),
                                  ALU.add).then_inc(banks_free, 1)

            def scale(dst, slab_end, index, lo):
                group_done(slab_end, index)
                dve.tensor_tensor(dst, psum(index % 2, L - lo), over(rstd, M, lo),
                                  ALU.mult).then_inc(banks_free, 1)

            def reciprocal(norm, lo):
                dve.wait_ge(root_ready, norm + 1)
                dve.reciprocal(rstd[:, lo:], rstd[:, lo:]).then_inc(rstd_ready, 1)
                dve.wait_ge(rstd_ready, norm + 1)

            def low_of(dst, src, high_t, wait, count, done):
                dve.wait_ge(wait, count)
                dve.tensor_tensor(dst, src, high_t.bitcast(F32), ALU.subtract).then_inc(done, 1)

            def relu_split(r, g, slab_end, index, parity, lo):
                group_done(slab_end, index)
                if lo == FROM2:
                    n = r - 4 * QUARTERS + 1
                    dve.wait_ge(low_half, n)
                    dve.tensor_tensor(act4[:, :, lo:], psum(parity, N2), act4[:, :, lo:],
                                      ALU.add).then_inc(banks_free, 1)
                    dve.wait_ge(banks_free, index + 1)
                    dve.scalar_tensor_tensor(act4[:, :, lo:], act4[:, :, lo:], 0.0, over(rstd, M, lo),
                                             ALU.max, ALU.mult).then_inc(joined, 1)
                else:
                    dve.scalar_tensor_tensor(act4[:, :, lo:], psum(parity, L - lo), 0.0, over(rstd, M, lo),
                                             ALU.max, ALU.mult).then_inc(banks_free, 1)
                low_of(tiles(hid[:, 1], g, lo), sq4[:, :, lo:], tiles(hid[:, 0], g, lo),
                       relu_high, r + 1, hid_ready)

            def split_channel_table():
                dve.wait_ge(table_high, 1)
                dve.tensor_tensor(tch[:, 1, :, :], raw_ch, tch[:, 0, :, :].bitcast(F32),
                                  ALU.subtract).then_inc(table_ready, 1)

            def split_sequence_table():
                dve.wait_ge(table_high, 2)
                dve.tensor_tensor(tseq[:, 1, :, 0:2, :], raw_seq, tseq[:, 0, :, 0:2, :].bitcast(F32),
                                  ALU.subtract).then_inc(table_ready, 1)
                dve.wait_ge(table_high, 3)
                dve.scalar_tensor_tensor(tseq[:, 1, :, 2, :], raw_seq[:, :, 1, :], -1.0,
                                         tseq[:, 0, :, 2, :].bitcast(F32), ALU.mult,
                                         ALU.subtract).then_inc(table_ready, 1)

            tap = glus = 0

            def more_taps(n, most=CONV_TILES * (TAPS - 1)):
                nonlocal tap
                n = max(0, min(n, most - tap))
                taps(tap, tap + n)
                tap += n

            def fill(n):
                more_taps(n, glus * 2 * (TAPS - 1))

            def glu(g, slab_end):
                scale(act4[:, :, :], slab_end, g, 0)
                slabs(slab_end, E - 1, E)
                fill(1)
                dve.wait_ge(glu_sig, g + 1)
                dve.tensor_tensor(conv_in[:, 2 * g:2 * g + 2, PAD:PAD + L], act4[:, 0:2, :], sq4[:, 0:2, :],
                                  ALU.mult).then_inc(glu_ready, 1)

            def split_u(g, slab_end):
                scale(act4[:, :, :], slab_end, 4 + g, 0)
                if g == 0:
                    slabs(slab_end, E - 1, E)
                fill(2)
                low_of(tiles(hid[:, 1], 2 + g, 0), act4[:, :, :], tiles(hid[:, 0], 2 + g, 0),
                       u_high, g + 1, u_ready)

            def taps(lo, hi):
                for n in range(lo, hi):
                    pair, step = divmod(n, 2 * (TAPS - 1))
                    tap, i = step // 2 + 1, step % 2
                    t = 2 * pair + i
                    w = par[:, C_CONV + t * TAPS + tap:C_CONV + t * TAPS + tap + 1]
                    if tap == 1:
                        dve.wait_ge(tap0_done, t + 1)
                    else:
                        dve.wait_ge(tap_done, n - 1)
                    dve.scalar_tensor_tensor(conv[:, t, FROM1:], conv_in[:, t, FROM1 + tap:FROM1 + tap + N1],
                                             w, conv[:, t, FROM1:], ALU.mult, ALU.add).then_inc(tap_done, 1)

            def split_v(hd):
                low_of(vs[0:TOK, hd % 2, 1, :, :], banks[0:TOK, ch_bank(hd):ch_bank(hd) + 3, 0:2 * HALF_DFT],
                       vs[0:TOK, hd % 2, 0, :, :], v_high, hd + 1, v_ready)

            def split_ya(hd):
                low_of(hid[:, 1, 2 * hd:2 * hd + 2, FROM1:], seq_psum(hd),
                       hid[:, 0, 2 * hd:2 * hd + 2, FROM1:], ya_high, hd + 1, ya_ready)

            def head_tiles(hd):
                return conv[:, 2 * hd:2 * hd + 2, FROM1:]

            def ln_centre(hd, bank):
                dve.wait_ge(ln_mean, hd + 1)
                mean = banks[:, bank, 0:N1].unsqueeze(1).broadcast_to([P, 2, N1])
                dve.scalar_tensor_tensor(head_tiles(hd), mean, -1.0 / HEAD_DIM, head_tiles(hd),
                                         ALU.mult, ALU.add).then_inc(ln_centred, 1)

            def ln_norm(hd):
                dve.wait_ge(ln_root, hd + 1)
                dve.reciprocal(ssum[:, hd, FROM1:], ssum[:, hd, FROM1:]).then_inc(ln_rstd, 1)
                dve.wait_ge(ln_rstd, hd + 1)
                dve.tensor_tensor(head_tiles(hd), head_tiles(hd), over(ssum[:, hd], 2, FROM1),
                                  ALU.mult).then_inc(ln_normed, 1)
                dve.wait_ge(ln_normed, hd + 1)

            def split_yb(hd):
                tiles_ = slice(KT // 2 + 2 * hd, KT // 2 + 2 * hd + 2)
                low_of(hid[:, 1, tiles_, FROM1:], head_tiles(hd), hid[:, 0, tiles_, FROM1:],
                       yb_high, hd + 1, yb_ready)

            E, EARLY = RING, 2

            dve.wait_ge(gains_landed, 16)
            split_x(0, 0, 0, 0, 2)
            slabs(0, 0, 1)
            split_x(0, 0, 0, 2, M)
            slabs(0, 1, 2)
            for q in range(1, KT // M):
                split_x(0, q, 0)
                slabs(0, 2 * q, 2 * q + 2)
            dve.wait_ge(squared, KT // M)
            dve.wait_ge(summed, 2)
            dve.tensor_tensor(ssum[:, :, :], ssum[:, :, :], sq4[:, :, :], ALU.add).then_inc(summed, 1)
            dve.wait_ge(summed, 3)
            dve.tensor_tensor(ssum[:, 0:2, :], ssum[:, 0:2, :], ssum[:, 2:4, :], ALU.add).then_inc(ssum_ready, 1)
            dve.wait_ge(ssum_ready, 1)
            dve.tensor_tensor(ssum[:, 0, :], ssum[:, 0, :], ssum[:, 1, :], ALU.add).then_inc(ssum_ready, 1)
            split_channel_table()
            slabs(SLABS, 0, EARLY)
            split_sequence_table()
            dve.wait_ge(consts_set, 4)
            dve.wait_ge(par_landed, 16)
            reciprocal(0, 0)

            for g in range(1, 6):
                for j in range(EARLY if g == 1 else 0, SLABS):
                    if j == E - 1:
                        glus = g - 1
                        if g == 1:
                            dve.wait_ge(table_ready, 3)
                        glu(g - 1, SLABS * g) if g < 5 else split_u(0, SLABS * g)
                    else:
                        slabs(SLABS * g, j, j + 1)
                        if g > 1 or j > E:
                            more_taps(4, 2 * (TAPS - 1) * (g if j > E else g - 1))
            ln_centre(0, 0)
            ln_centre(1, 1)
            more_taps(10)
            split_u(1, S_OUT_A)
            more_taps(2)
            split_v(0)
            more_taps(6)
            slabs(S_OUT_A, 0, 1)
            split_v(1)
            more_taps(1)
            split_ya(0)
            ln_norm(0)
            split_v(2)
            slabs(S_OUT_A, 1, 2)
            more_taps(2)
            split_ya(1)
            ln_norm(1)
            split_v(3)
            split_yb(0)
            more_taps(4)
            slabs(S_OUT_A, 2, 3)
            split_ya(2)
            slabs(S_OUT_A, 3, RING)
            split_yb(1)
            more_taps(6)
            split_ya(3)
            more_taps(5)
            for s in range(4, 21):
                if s in (9, 14):
                    n = s // 14
                    residual(n, S_OUT_A + 6 * (n + 1), G_OUT_A + n, n % 2, FROM1)
                slabs(S_OUT_A, s, s + 1)
                if s == 17:
                    ln_centre(2, M)
                more_taps(2 if s in (9, 14) else 4 + s % 2)
            more_taps(CONV_TILES * (TAPS - 1))
            residual(2, S_OUT_A + 18, G_OUT_A + 2, 0, FROM1)
            slabs(S_OUT_A, 21, 22)
            ln_centre(3, 0)
            slabs(S_OUT_A, 22, 23)
            ln_norm(2)
            slabs(S_OUT_A, 23, 24)
            ln_norm(3)
            slabs(S_OUT_A, 24, 25)
            split_yb(2)
            slabs(S_OUT_A, 25, 26)
            split_yb(3)
            slabs(S_OUT_A, 26, 27)
            residual(3, S_OUT_B, G_OUT_A + 3, 1, FROM1)
            slabs(S_OUT_A, 27, 29)
            residual(0, S_OUT_B + 2, G_OUT_B, 0, FROM1)
            slabs(S_OUT_A, 29, 30)
            split_x(1, 0, FROM1)
            slabs(S_OUT_A, 30, 31)
            residual(1, S_OUT_B + 4, G_OUT_B + 1, 1, FROM1)
            slabs(S_OUT_A, 31, 32)
            split_x(1, 1, FROM1)

            def mlp(slab0, norm, lo, index0, r0, next_norm, next_lo, prev_lo):
                def quarter(q, first=False, last=False):
                    s0, r, i0 = q * SQ + slab0, q * 4 + r0, q * GQ + index0
                    for g in range(GQ):
                        if g == 0 and first and norm == 1:
                            slabs(s0, 0, 1)
                            residual(2, s0 - 2, i0 - 2, 0, lo)
                            slabs(s0, 1, 2)
                            split_x(norm, 2, lo)
                            slabs(s0, 2, E)
                        else:
                            slabs(s0, SLABS * g + (EARLY if g == 1 and first else 0), SLABS * g + E)
                        end, index, parity = s0 + SLABS * g, i0 + (g - 1), (g - 1) % 2
                        if g == 0:
                            residual(3, end, index, parity, prev_lo if first else lo, q * 4 + 3)
                            if first:
                                split_x(norm, 3, lo)
                        elif g <= 4:
                            relu_split(r + (g - 1), g - 1, end, index, parity, lo)
                        else:
                            residual(g - 5, end, index, parity, lo, q * 4 + (g - 1))
                            if last and next_norm < 4:
                                split_x(next_norm, g - 5, next_lo)
                        slabs(s0, SLABS * g + E, SLABS * g + SLABS)
                        if g == 0 and first:
                            slabs(s0, SLABS, SLABS + EARLY)
                            reciprocal(norm, lo)
                quarter(0, first=True)
                with dve.Fori(1, QUARTERS - 1) as q:
                    quarter(q)
                quarter(QUARTERS - 1, last=True)

            mlp(S_MLP0, 1, FROM1, G_MLP0, 0, 2, FROM1, FROM1)

            def short_conv(j):
                for tap_ in range(3):
                    for i in range(M):
                        c = C_SHORT + (M * j + i) * 3 + tap_
                        n = 3 * M * j + M * tap_ + i
                        dst, src = short_out[:, i, :], short_in[:, i, tap_ + 1:tap_ + 1 + N2]
                        if tap_ == 0:
                            dve.tensor_scalar(dst, src, par[:, c:c + 1], None, ALU.mult).then_inc(short_tap, 1)
                        else:
                            dve.wait_ge(short_tap, n - M + 1)
                            dve.scalar_tensor_tensor(dst, src, par[:, c:c + 1], dst, ALU.mult,
                                                     ALU.add).then_inc(short_tap, 1)

            def gated(j, slab_end, index):
                scale(act4[:, :, FROM1:], slab_end, index, FROM1)
                dve.wait_ge(short_tap, 3 * M * (j + 1))
                dve.wait_ge(banks_free, index + 1)
                dve.tensor_tensor(short_out, short_out, act4[:, :, FROM2:], ALU.mult).then_inc(y_ready, 1)
                low_of(tiles(hid[:, 1], j, FROM2), short_out, tiles(hid[:, 0], j, FROM2),
                       y_high, j + 1, gated_ready)

            for i in range(4):
                for k in range(3):
                    s0, index = S_C_IN + SLABS * (3 * i + k), G_C_IN + 3 * i + k - 1
                    slabs(s0, EARLY if k == 1 and i == 0 else 0, E)
                    if k == 0 and i == 0:
                        residual(3, s0, index, index % 2, FROM1)
                        split_x(2, 3, FROM1)
                        dve.memset(conv_in[:, 0:M, N1:N1 + 1], 0.0).then_inc(consts_set, 1)
                        dve.wait_ge(consts_set, 5)
                    elif k == 0:
                        gated(i - 1, s0, index)
                    elif k == 1:
                        scale(gate_c, s0, index, FROM1)
                    else:
                        scale(act4[:, :, FROM1:], s0, index, FROM1)
                        dve.wait_ge(banks_free, index + 1)
                        dve.tensor_tensor(short_in[:, :, 0:N1], act4[:, :, FROM1:], gate_c,
                                          ALU.mult).then_inc(short_ready, 1)
                    if k == 2:
                        slabs(s0, E, E + 2)
                        dve.wait_ge(short_ready, i + 1)
                        short_conv(i)
                        slabs(s0, E + 2, SLABS)
                    else:
                        slabs(s0, E, SLABS)
                    if k == 0 and i == 0:
                        slabs(s0, SLABS, SLABS + EARLY)
                        reciprocal(2, FROM1)
            for g in range(4):
                s0 = S_C_OUT + SLABS * g
                slabs(s0, 0, E)
                if g == 0:
                    gated(3, s0, G_C_OUT - 1)
                else:
                    residual(g - 1, s0, G_C_OUT + g - 1, (g - 1) % 2, FROM2, g - 1)
                    split_x(3, g - 1, FROM2)
                slabs(s0, E, SLABS)

            mlp(S_MLP1, 3, FROM2, G_MLP1, 4 * QUARTERS, 4, FROM2, FROM2)
            group_done(S_END, G_END - 1)
            for n in range(2):
                t = slice(KT - M + 2 * n, KT - M + 2 * n + 2)
                for at in (N2, 0):
                    if at == 0:
                        dve.wait_ge(tail_added, n + 1)
                    add = dve.tensor_tensor(h[:, t, FROM2:], h[:, t, FROM2:],
                                            banks[:, M + 2 * n:M + 2 * n + 2, at:at + N2], ALU.add)
                    add.then_inc(joined if at == 0 else tail_added, 1)
            reciprocal(4, FROM2)
            for t in range(0, KT - M, 2):
                dve.wait_ge(scaled, t + 2)
                dve.tensor_tensor(h[:, t:t + 2, FROM2:], h[:, t:t + 2, FROM2:], over(rstd, 2, FROM2),
                                  ALU.mult).then_inc(normed, 2)
            for t in range(KT - M, KT):
                dve.scalar_tensor_tensor(h[:, t, FROM2:], h[:, t, FROM2:], gain(4, t), rstd[:, FROM2:],
                                         ALU.mult, ALU.mult).then_inc(normed, 1)


def dft_tables():
    c = np.arange(HEAD_DIM)
    angle = 2 * np.pi * (np.outer(c, c[:HALF_DFT]) % HEAD_DIM) / HEAD_DIM
    ch = np.concatenate([np.cos(angle), np.sin(angle)], 1) / np.sqrt(HEAD_DIM)
    ch = ch.reshape(2, P, 2 * HALF_DFT).transpose(1, 0, 2)
    t = np.arange(L)
    angle = 2 * np.pi * (np.outer(t, t[FROM1:]) % L) / L
    seq = np.stack([np.cos(angle), -np.sin(angle)], 1) / np.sqrt(L)
    parts = []
    for n, at in enumerate(TOK_AT):
        part = seq[at:at + TOK].copy()
        if n == 2:
            part[:TOK_AT[1] + TOK - at] = 0.0
        parts.append(part)
    return ch.astype(np.float32), np.stack(parts, 1).astype(np.float32)


def chunked(w, k0, k1, cols):
    part = np.concatenate([w[k0:k1, a:b] for a, b in cols], 1)
    n = (k1 - k0) // (P * CHUNK_K)
    return part.reshape(n, CHUNK_K, P, COLS).transpose(0, 2, 1, 3).reshape(n, P, CHUNK_K * COLS)


def weight_chunks(ab_w_in, ab_w_out, c_w_in, c_w_out, mlp_w1, mlp_w2):
    def span(n, at=0):
        return [(at + COLS * n, at + COLS * n + COLS)]

    def mlp(w1, w2):
        for q in range(QUARTERS):
            for g in range(4):
                yield chunked(w1, 0, D, span(g, D * q))
            for g in range(4):
                yield chunked(w2, D * q, D * q + D, span(g))

    half = D // 2
    out = []
    for g in range(4):
        a, b = half + COLS // 2 * g, 2 * half + COLS // 2 * g
        out.append(chunked(ab_w_in[0], 0, D, [(a, a + COLS // 2), (b, b + COLS // 2)]))
    for g in range(2):
        out.append(chunked(ab_w_in[0], 0, D, span(g)))
    rows = np.arange(D).reshape(-1, 2, P)
    rows[:HEADS, 1] = rows[:HEADS, 1, ::-1]
    w_out = ab_w_out[0][rows.reshape(-1)]
    for k in ((0, half * 3 // 2), (half * 3 // 2, D)):
        for g in range(4):
            out.append(chunked(w_out, *k, span(g)))
    out += mlp(mlp_w1[0], mlp_w2[0])
    for j in range(4):
        out += [chunked(c_w_in[0], 0, D, span(j, at)) for at in (D, 2 * D, 0)]
    for g in range(4):
        out.append(chunked(c_w_out[0], 0, D, span(g)))
    out += mlp(mlp_w1[1], mlp_w2[1])
    return np.concatenate(out)


def packed_params(norms, conv_w, conv_b, ln_g, ln_b, short_w):
    cols = [n.reshape(KT, P).T for n in norms]
    cols.append(conv_w.reshape(TAPS, CONV_TILES, P).transpose(2, 1, 0).reshape(P, -1))
    cols += [v.reshape(CONV_TILES, P).T for v in (conv_b, ln_g, ln_b)]
    cols.append(short_w.reshape(3, KT, P).transpose(2, 1, 0).reshape(P, -1))
    return np.concatenate(cols, 1)


def kernel(**inputs):
    import concourse.bacc as bacc
    from concourse.bass_utils import run_bass_kernel_spmd

    a = {k: np.asarray(v) for k, v in inputs.items()}
    tokens = np.concatenate([a["meta_tokens"], a["x"][0]], 0)
    ch, seq = dft_tables()
    arrays = {
        "weights": weight_chunks(a["ab_w_in"], a["ab_w_out"], a["c_w_in"], a["c_w_out"],
                                 a["mlp_w1"], a["mlp_w2"]),
        "x": np.ascontiguousarray(tokens.T.reshape(KT, P, L).transpose(1, 0, 2)),
        "params": packed_params([a["norm_mix_g"][0], a["norm_mlp_g"][0], a["norm_mix_g"][1],
                                 a["norm_mlp_g"][1], a["norm_final_g"]], a["ab_conv_w"][0],
                                a["ab_conv_b"][0], a["ab_ln_g"][0], a["ab_ln_b"][0], a["c_conv_w"][0]),
        "dft_ch": ch,
        "dft_seq": seq,
    }
    nc = bacc.Bacc("TRN2", target_bir_lowering=False, num_devices=1)
    aps = {n: nc.dram_tensor(n, v.shape, F32, kind="ExternalInput").ap() for n, v in arrays.items()}
    out = nc.dram_tensor("out", (P, KT, SEQ), F32, kind="ExternalOutput").ap()
    trunk(nc, aps["weights"], aps["x"], aps["params"], aps["dft_ch"], aps["dft_seq"], out)
    r = run_bass_kernel_spmd(nc, [arrays], core_ids=[0])
    y = r.results[0]["out"]
    return np.ascontiguousarray(y.transpose(1, 0, 2).reshape(D, SEQ).T)[None]
```
